# Optimizing a Trainium2 kernel written in Bass

```python
import math
import jax, jax.numpy as jnp
from jax import lax
import numpy as np

D_MODEL = 1024
BATCH = 1
SEQ = 1024
DEPTH = 2

N_MIXERS = 2
POOL_WINDOWS = (2, 4, 8, 16)
POOL_GROUPS = len(POOL_WINDOWS)
POOL_GROUP_DIM = D_MODEL // POOL_GROUPS
RET_HEADS = 4
RET_QK_DIM = D_MODEL // RET_HEADS
RET_V_DIM = 2 * D_MODEL // RET_HEADS
RET_QK_TOTAL = RET_HEADS * RET_QK_DIM
RET_V_TOTAL = RET_HEADS * RET_V_DIM
RET_IN_DIM = 2 * RET_QK_TOTAL + 2 * RET_V_TOTAL
RET_CHUNK = 128
ROPE_BASE = 10000.0
D_FF = 2816
CONV_WIDTH = 3
EPS = 1e-6
N_NORMS = 4
N_POOL_LAYERS = (DEPTH + N_MIXERS - 1) // N_MIXERS
N_RET_LAYERS = DEPTH // N_MIXERS

kernel_name = "hybrid_pool_retention_convglu"

def rms_norm(x, gain):
    xf = x.astype(jnp.float32)
    var = jnp.mean(xf * xf, axis=-1, keepdims=True)
    return (xf * lax.rsqrt(var + EPS) * gain.astype(jnp.float32)).astype(x.dtype)

def pool_mixer(h, w_groups, scale):
    b, s, d = h.shape
    hf = h.astype(jnp.float32)
    cs = jnp.cumsum(hf, axis=1)
    t = jnp.arange(s)
    parts = []
    for g, win in enumerate(POOL_WINDOWS):
        lo, hi = g * POOL_GROUP_DIM, (g + 1) * POOL_GROUP_DIM
        c = cs[..., lo:hi]
        c_shift = jnp.pad(c, ((0, 0), (win, 0), (0, 0)))[:, :s]
        count = jnp.minimum(t + 1, win).astype(jnp.float32)[None, :, None]
        parts.append((c - c_shift) / count - hf[..., lo:hi])
    diff = jnp.concatenate(parts, axis=-1).reshape(b, s, POOL_GROUPS, POOL_GROUP_DIM)
    y = jnp.einsum('bsgc,gcd->bsgd', diff, w_groups.astype(jnp.float32)).reshape(b, s, d)
    return (y * scale.astype(jnp.float32)).astype(h.dtype)

def rotary(x, positions):
    dh = x.shape[-1]
    inv_freq = ROPE_BASE ** (-jnp.arange(0, dh, 2, dtype=jnp.float32) / dh)
    ang = positions.astype(jnp.float32)[..., None] * inv_freq
    cos = jnp.cos(ang)[:, :, None, :]
    sin = jnp.sin(ang)[:, :, None, :]
    x1, x2 = x[..., : dh // 2], x[..., dh // 2:]
    return jnp.concatenate([x1 * cos - x2 * sin, x2 * cos + x1 * sin], axis=-1)

def retention(h, positions, w_in, gn_gain, w_out):
    b, s, _ = h.shape
    n_chunks = s // RET_CHUNK
    proj = (h @ w_in).astype(jnp.float32)
    q, k, v, g = jnp.split(proj, [RET_QK_TOTAL, 2 * RET_QK_TOTAL, 2 * RET_QK_TOTAL + RET_V_TOTAL], axis=-1)
    q = rotary(q.reshape(b, s, RET_HEADS, RET_QK_DIM), positions) * (RET_QK_DIM ** -0.5)
    k = rotary(k.reshape(b, s, RET_HEADS, RET_QK_DIM), positions)
    v = v.reshape(b, s, RET_HEADS, RET_V_DIM)

    def to_chunks(a):
        return a.reshape(b, n_chunks, RET_CHUNK, RET_HEADS, a.shape[-1]).transpose(1, 0, 3, 2, 4)

    qc, kc, vc = to_chunks(q), to_chunks(k), to_chunks(v)

    log_gamma = jnp.log(1.0 - 2.0 ** (-5.0 - jnp.arange(RET_HEADS, dtype=jnp.float32)))
    i = jnp.arange(RET_CHUNK, dtype=jnp.float32)
    rel = i[:, None] - i[None, :]
    intra_decay = jnp.where(rel >= 0, jnp.exp(jnp.maximum(rel, 0.0) * log_gamma[:, None, None]), 0.0)
    cross_decay = jnp.exp((i + 1.0) * log_gamma[:, None])[None, :, :, None]
    in_decay = jnp.exp((RET_CHUNK - 1.0 - i) * log_gamma[:, None])[None, :, :, None]
    chunk_decay = jnp.exp(RET_CHUNK * log_gamma)[None, :, None, None]

    def step(state, xs):
        qb, kb, vb = xs
        scores = jnp.einsum('bhid,bhjd->bhij', qb, kb) * intra_decay[None]
        out = jnp.einsum('bhij,bhjv->bhiv', scores, vb) \
            + jnp.einsum('bhid,bhdv->bhiv', qb, state) * cross_decay
        state = state * chunk_decay + jnp.einsum('bhjd,bhjv->bhdv', kb * in_decay, vb)
        return state, out

    state0 = jnp.zeros((b, RET_HEADS, RET_QK_DIM, RET_V_DIM), jnp.float32)
    _, o = lax.scan(step, state0, (qc, kc, vc))
    o = o.transpose(1, 0, 3, 2, 4).reshape(b, s, RET_HEADS, RET_V_DIM)
    mu = jnp.mean(o, axis=-1, keepdims=True)
    var = jnp.mean(jnp.square(o - mu), axis=-1, keepdims=True)
    o = ((o - mu) * lax.rsqrt(var + EPS)).reshape(b, s, RET_V_TOTAL) * gn_gain.astype(jnp.float32)
    y = jax.nn.silu(g) * o
    return (y.astype(h.dtype) @ w_out)

def conv_glu(h, w_up, conv_w, conv_b, w_down):
    s = h.shape[1]
    u = h @ w_up
    up = jnp.pad(u, ((0, 0), (CONV_WIDTH - 1, 0), (0, 0)))
    c = conv_b
    for tap in range(CONV_WIDTH):
        c = c + up[:, tap:tap + s] * conv_w[tap]
    gate, val = jnp.split(c, 2, axis=-1)
    return (jax.nn.silu(gate) * val) @ w_down

def setup_inputs(seed: int = 0) -> dict:
    key = jax.random.key(seed)
    ks = jax.random.split(key, 14)
    f32 = jnp.float32
    x = jax.random.normal(ks[0], (BATCH, SEQ, D_MODEL), f32)
    offsets = jax.random.randint(ks[1], (BATCH, 1), 0, 1024, dtype=jnp.int32)
    positions = (jnp.arange(SEQ, dtype=jnp.int32)[None, :] + offsets).astype(jnp.int32)
    norm_gain = 1.0 + 0.05 * jax.random.normal(ks[2], (DEPTH, N_NORMS, D_MODEL), f32)
    pool_w = jax.random.normal(ks[3], (N_POOL_LAYERS, POOL_GROUPS, POOL_GROUP_DIM, POOL_GROUP_DIM), f32) * POOL_GROUP_DIM ** -0.5
    pool_scale = 1.0 + 0.1 * jax.random.normal(ks[4], (N_POOL_LAYERS, D_MODEL), f32)
    ret_w_in = jax.random.normal(ks[5], (N_RET_LAYERS, D_MODEL, RET_IN_DIM), f32) * D_MODEL ** -0.5
    ret_gn_gain = 1.0 + 0.05 * jax.random.normal(ks[6], (N_RET_LAYERS, RET_V_TOTAL), f32)
    ret_w_out = jax.random.normal(ks[7], (N_RET_LAYERS, RET_V_TOTAL, D_MODEL), f32) * RET_V_TOTAL ** -0.5
    mlp_w_up = jax.random.normal(ks[8], (DEPTH, D_MODEL, 2 * D_FF), f32) * D_MODEL ** -0.5
    mlp_conv_w = jax.random.normal(ks[9], (DEPTH, CONV_WIDTH, 2 * D_FF), f32) * CONV_WIDTH ** -0.5
    mlp_conv_b = 0.02 * jax.random.normal(ks[10], (DEPTH, 2 * D_FF), f32)
    mlp_w_down = jax.random.normal(ks[11], (DEPTH, D_FF, D_MODEL), f32) * D_FF ** -0.5
    return {"x": x, "positions": positions, "norm_gain": norm_gain,
            "pool_w": pool_w, "pool_scale": pool_scale,
            "ret_w_in": ret_w_in, "ret_gn_gain": ret_gn_gain, "ret_w_out": ret_w_out,
            "mlp_w_up": mlp_w_up, "mlp_conv_w": mlp_conv_w, "mlp_conv_b": mlp_conv_b,
            "mlp_w_down": mlp_w_down}

def reference(x, positions, norm_gain, pool_w, pool_scale, ret_w_in, ret_gn_gain,
              ret_w_out, mlp_w_up, mlp_conv_w, mlp_conv_b, mlp_w_down):
    for layer in range(DEPTH):
        gains = norm_gain[layer]
        h = rms_norm(x, gains[0])
        j = layer // N_MIXERS
        if layer % N_MIXERS == 0:
            m = pool_mixer(h, pool_w[j], pool_scale[j])
        else:
            m = retention(h, positions, ret_w_in[j], ret_gn_gain[j], ret_w_out[j])
        x = x + rms_norm(m, gains[1])
        h = rms_norm(x, gains[2])
        f = conv_glu(h, mlp_w_up[layer], mlp_conv_w[layer], mlp_conv_b[layer], mlp_w_down[layer])
        x = x + rms_norm(f, gains[3])
    return x


_drawn_inputs = setup_inputs


def setup_inputs(seed=0):
    import zlib

    import numpy as np

    out = dict(_drawn_inputs(seed))
    spreads = {}
    factors = {}
    for name, (base, spread) in spreads.items():
        noise = np.random.default_rng([zlib.crc32(name.encode()), seed]).standard_normal(out[name].shape)
        drawn = base * np.exp(spread * noise) if base else spread * noise
        out[name] = __import__('jax').numpy.asarray(drawn.astype(out[name].dtype))
    for name, factor in factors.items():
        out[name] = (out[name] * factor).astype(out[name].dtype)
    return out
```

```python
from contextlib import ExitStack, contextmanager

import concourse.bass as bass
from concourse import mybir
import numpy as np

ALU = mybir.AluOpType
ACT = mybir.ActivationFunctionType
F32 = mybir.dt.float32
F32R = mybir.dt.float32r
BF16 = mybir.dt.bfloat16
I32 = mybir.dt.int32

P = 128
HALF = 512
WINDOWS = (2, 4, 8, 16)
HEADS = 4
CHUNKS_UP = 4
EPS = 1e-6
ROUND = 12582912.0
TURNS = 4096.0
NEWEST = (4, 6, 0, 2)


def two_pi_parts():
    rest, parts = 2.0 * np.pi, []
    for _ in range(2):
        scale = 2.0 ** (11 - np.floor(np.log2(abs(rest))))
        part = np.round(rest * scale) / scale
        parts.append(float(part))
        rest -= part
    return parts + [float(np.float32(rest))]


def shape_constants(seq):
    s, t = np.arange(P)[:, None], np.arange(P)[None, :]
    first, main, prev = [], [], []
    for win in WINDOWS:
        inside = (s <= t) & (s > t - win)
        count = np.minimum(t + 1, win)
        first.append(inside / count - (s == t))
        main.append(inside / win - (s == t))
        w = np.arange(max(WINDOWS))[None, :]
        prev.append((s - P > w - win) / win)
    pool = np.concatenate(first + main + prev, axis=1).astype(np.float32)
    log_gamma = np.log(1.0 - 2.0 ** (-5.0 - np.arange(HEADS)))
    tok = np.arange(seq).reshape(-1, P).T
    qk_dim = 2 * P
    out_decay = np.exp(tok[:, None, :] * log_gamma[None, :, None]) * qk_dim ** -0.5
    v_decay = np.exp(-tok[:, None, :] * log_gamma[None, :, None])
    inv_freq = 10000.0 ** (-np.arange(P) / P)
    small = np.concatenate([
        np.eye(P), (s <= t),
        out_decay.reshape(P, -1), v_decay.reshape(P, -1), inv_freq[:, None],
    ], axis=1).astype(np.float32)
    return pool, small


class Tally:

    def __init__(self, eng, sem):
        self.eng, self.sem, self.base, self.local = eng, sem, 0, 0

    def mark(self, ins):
        ins.then_inc(self.sem, 1)
        self.local += 1

    def wait(self, but=0):
        self.eng.wait_ge(self.sem, self.base + self.local - but)


@contextmanager
def turns(eng, count, tally=None, per_turn=0):
    before = tally.base + tally.local if tally else 0
    with eng.Fori(0, count) as i:
        if tally:
            tally.base, tally.local = before + i * per_turn, 0
        yield i
        if tally:
            assert tally.local == per_turn, (tally.local, per_turn)
    if tally:
        tally.base, tally.local = before + count * per_turn, 0


def hybrid_trunk(nc, x, positions, norm_gain, pool_w, pool_scale, ret_w_in, ret_gn_gain, ret_w_out,
                 mlp_w_up, mlp_conv_w, mlp_conv_b, mlp_w_down, pool_tables, small_tables, out):
    seq, d = x.shape[1], x.shape[2]
    KT = d // P
    TT = seq // P
    TH = TT // 2
    dff = mlp_w_down.shape[1]
    FT = dff // P
    VT = ret_w_out.shape[1] // P
    HV = VT // HEADS
    G = len(WINDOWS)
    GC = KT // G
    GW = d // G
    WMAX = max(WINDOWS)
    qk_total = HEADS * 2 * P
    v_total = VT * P
    assert (seq, d, KT, TT) == (2 * HALF, 1024, 8, 8) and FT % 2 == 0

    UP = 2 * FT
    HEAD_SLICES = 12
    up0, down0 = 0, UP
    ret0 = down0 + 2 * FT
    out0 = ret0 + HEADS * HEAD_SLICES
    up1 = out0 + 2 * VT
    down1 = up1 + UP
    n_slices = down1 + 2 * FT

    ctx = ExitStack()
    with ctx:
        base = (nc.sbuf_base + 31) // 32 * 32
        arena = nc.sbuf_usable_end - base
        KB = 1024
        off = {}
        at = base
        for name, size in (("A", 64 * KB), ("G", 88 * KB), ("raw", 16 * KB), ("w", 16 * KB), ("T", 16 * KB)):
            off[name] = at
            at += size

        def place(name, shape, dt, region, byte=0):
            return nc.alloc_sbuf_tensor_at(name, shape, dt, offset=off[region] + byte)

        TILE = 4 * KB
        a_hi = place("a_hi", [P, 2, KT, HALF], F32R, "A")
        a_lo = place("a_lo", [P, 2, KT, HALF], F32R, "A", 32 * KB)
        y_st0 = place("y_st0", [P, TH, d], F32, "A", 16 * KB)
        x_st0 = place("x_st0", [P, TH, d], F32, "A", 48 * KB)
        g_t = place("g_t", [P, FT, seq], F32, "G")
        y_st1 = place("y_st1", [P, TH, d], F32, "G")
        x_st1 = place("x_st1", [P, TH, d], F32, "G", 8 * TILE)
        x_p = place("x_p", [P, TT, d], F32, "G")
        h0 = place("h0", [P, 4, d], F32, "G", 8 * TILE)
        y_stp = place("y_stp", [P, 4, d], F32, "G", 12 * TILE)
        pw_raw = place("pw_raw", [P, KT, GW], F32, "G", 12 * TILE)
        pw_hi = place("pw_hi", [P, KT, GW], F32R, "G", 16 * TILE)
        pw_lo = place("pw_lo", [P, KT, GW], F32R, "G", 18 * TILE)
        par_rows = place("par_rows", [P, 8, P], F32, "G", 14 * TILE)
        gn_rows = place("gn_rows", [P, P], F32, "G", 15 * TILE)
        gain_first = place("gain_first", [P, d], F32, "G", 20 * TILE)
        pool_scale_b = place("pool_scale_b", [P, d], F32, "G", 21 * TILE)
        q_s = place("q_s", [P, 2, 2, 2, HALF], F32R, "G")
        o_s = place("o_s", [P, TT, HALF], F32, "G")
        k_s = place("k_s", [P, 2, 2, 2, HALF], F32R, "G", 4 * TILE)
        v_hi = place("v_hi", [P, TT, HALF], F32R, "G", 8 * TILE)
        v_lo = place("v_lo", [P, TT, HALF], F32R, "G", 12 * TILE)
        s_hi = place("s_hi", [P, 2, HALF], F32R, "G", 16 * TILE)
        s_lo = place("s_lo", [P, 2, HALF], F32R, "G", 17 * TILE)
        cos_t = place("cos_t", [P, seq], F32, "G", 20 * TILE)
        sin_t = place("sin_t", [P, seq], F32, "G", 21 * TILE)
        ang_a = place("ang_a", [P, seq], F32, "G", 16 * TILE)
        ang_b = place("ang_b", [P, seq], F32, "G", 17 * TILE)
        ang_c = place("ang_c", [P, seq], F32, "G", 18 * TILE)
        pos_i = place("pos_i", [P, seq], I32, "G", 19 * TILE)
        w_raw = place("w_raw", [P, 4, d], F32, "raw")
        w_hi = place("w_hi", [P, 2, d], F32R, "w")
        w_lo = place("w_lo", [P, 2, d], F32R, "w", 8 * KB)
        conv = place("conv", [P, 2, seq], F32, "T")
        junk = place("junk", [P, d], BF16, "T")
        gain_post = place("gain_post", [P, d], F32, "T", 4 * KB)
        gs_hi = place("gs_hi", [P, 2, HALF], F32R, "T", 8 * KB)
        gs_lo = place("gs_lo", [P, 2, HALF], F32R, "T", 12 * KB)
        pool_m = place("pool_m", [P, pool_tables.shape[1]], F32, "T", 8 * KB)
        rot = place("rot", [P, 4, seq], F32, "T")
        gate = place("gate", [P, HV, seq], F32, "T")
        off["C"] = at
        gain_pre = place("gain_pre", [P, d], F32, "C")
        small = place("small", [P, small_tables.shape[1]], F32, "C", 4 * KB)
        at += 4 * KB + (small_tables.shape[1] * 4 + 31) // 32 * 32
        off["D"] = at
        taps = place("taps", [P, 2, 4, UP], F32, "D")
        at += 2 * 4 * UP * 4
        off["E"] = at
        gn_gain = place("gn_gain", [P, VT], F32, "E")
        stat = place("stat", [P, TT, 8], F32, "E", 64)
        bn6 = place("bn6", [P, TT, 6], F32, "E", 64 + 256)
        mv = place("mv", [P, TT, 2], F32, "E", 64 + 256 + 192)
        gn_root = place("gn_root", [P, TT], F32, "E", 64 + 256 + 192 + 64)
        gn_rstd = place("gn_rstd", [P, TT], F32, "E", 64 + 256 + 192 + 96)
        flag_t = place("flag_t", [P, 1], F32, "E", 64 + 256 + 192 + 128)
        assert at + 64 + 256 + 192 + 160 <= base + arena, (at, base, arena)

        ident = small[:, 0:P]
        causal = small[:, P:2 * P]
        nd = HEADS * TT
        out_decay = small[:, 2 * P:2 * P + nd]
        v_decay = small[:, 2 * P + nd:2 * P + 2 * nd]
        inv_freq = small[:, 2 * P + 2 * nd:2 * P + 2 * nd + 1]

        ps = ctx.enter_context(nc.psum_tensor("ps", [P, 8, HALF], F32))

        def pair(b):
            return ps[:, b:b + 2, :].rearrange("p b n -> p (b n)")

        x_scr = nc.dram_tensor("x_scratch", (TT, P, d), F32).ap()
        y_scr = nc.dram_tensor("y_scratch", (VT, P, seq), F32).ap()

        def sem(name):
            return ctx.enter_context(nc.semaphore(name))

        raw_full = [sem(f"raw_full{j}") for j in range(4)]
        w_hi_done, w_split = sem("w_hi_done"), sem("w_split")
        slice_done = sem("slice_done")
        tap_done, conv_done, silu_done, mult_done = (sem(n) for n in ("tap_done", "conv_done", "silu_done", "mult_done"))
        gs_hi_done, gs_split = sem("gs_hi_done"), sem("gs_split")
        y_done, drained_a, drained_v = sem("y_done"), sem("drained_a"), sem("drained_v")
        y_root, x1_done, x_root, h_done = (sem(n) for n in ("y_root", "x1_done", "x_root", "h_done"))
        tr_done, a_hi_done, a_done = sem("tr_done"), sem("a_hi_done"), sem("a_done")
        x_first = [sem(f"x_first{t}") for t in range(TT)]
        x_in = [sem(f"x_in{t}") for t in range(TT)]
        x_stored = [sem("x_stored0"), sem("x_stored1")]
        gain_in, const_in, par_done, eps_done = sem("gain_in"), sem("const_in"), sem("par_done"), sem("eps_done")
        x0_root, h0_done, pool_done, d_hi_done, d_split = (
            sem(n) for n in ("x0_root", "h0_done", "pool_done", "d_hi_done", "d_split"))
        pw_scaled, pw_hi_done, pw_split, pool_in = (sem(n) for n in ("pw_scaled", "pw_hi_done", "pw_split", "pool_in"))
        pos_in, ang_done, sin_done = sem("pos_in"), sem("ang_done"), sem("sin_done")
        rot_copied, rot_f32, rot_hi, rot_split = (sem(n) for n in ("rot_copied", "rot_f32", "rot_hi", "rot_split"))
        v_done, v_hi_done, v_split = sem("v_done"), sem("v_hi_done"), sem("v_split")
        s_done, s_hi_done, s_split = sem("s_done"), sem("s_hi_done"), sem("s_split")
        o_done, o_copied = sem("o_done"), sem("o_copied")
        gate_done, gn_var, gn_root_done, gn_done = (sem(n) for n in ("gate_done", "gn_var", "gn_root_done", "gn_done"))
        ot_done, yt_done, yt_stored, gate_free = (sem(n) for n in ("ot_done", "yt_done", "yt_stored", "gate_free"))
        y_back = [sem(f"y_back{h}") for h in range(HEADS)]
        out_done = sem("out_done")
        act_chain, dve_chain, pool_chain = sem("act_chain"), sem("dve_chain"), sem("pool_chain")

        LAST = 3

        def plan_steps(nk, half, sub):
            lead = 2 * TH if half == 1 else (nk - 2 if sub == 2 else 0)
            n_loop = (nk - 2 - lead) // 4
            return nk - 2 - 4 * n_loop, n_loop

        def y_pos(f):
            return VT + 3 - f

        def a_cols(a, t):
            return a[:, t // TH, :, (t % TH) * P:(t % TH + 1) * P]

        def f32(ap):
            return ap.bitcast(F32)

        block = ctx.enter_context(nc.Block())

        @block.sync
        def _(sp):
            def load(s, src, slot, first=False):
                if not first:
                    sp.wait_ge(w_split, s - 3)
                sp.dma_start(src[0](w_raw[:, slot, :]), src[1]).then_inc(raw_full[slot], 16)

            def flat(ap):
                return ap

            def columns(w, c0):
                return (lambda r: r.rearrange("p (k n) -> p k n", k=KT),
                        w.rearrange("(k p) n -> p k n", p=P)[:, :, c0])

            def up_load(layer, i, z, s, slot, first=False):
                load(s, columns(mlp_w_up[layer], bass.ds(z * dff + i * P, P)), slot, first)

            def mlp(layer, up_base, down_base):
                def four(i0, s0, first=False):
                    for u in range(4):
                        up_load(layer, i0 + u // 2, u % 2, s0 + u, u, first)
                if up_base == 0:
                    four(0, 0, True)
                    with turns(sp, FT // 2 - 1) as i:
                        four(2 * i + 2, 4 * i + 4)
                else:
                    with turns(sp, FT // 2) as i:
                        four(2 * i, 4 * i + up_base)
                down(mlp_w_down[layer], down_base, FT)

            def down(w, down_base, nk):
                rows = w.rearrange("(k p) n -> k p n", p=P)
                for half in range(2):
                    s0 = down_base + half * nk
                    lead = nk % 4
                    for k in range(lead):
                        load(s0 + k, (flat, rows[k]), (s0 + k) % 4)
                    with turns(sp, nk // 4) as i:
                        for u in range(4):
                            src = rows[bass.ds(lead + 4 * i + u, 1)].rearrange("o p n -> p (o n)")
                            load(s0 + lead + 4 * i + u, (flat, src), (s0 + lead + u) % 4)

            for t in range(TT):
                sp.dma_start(x_p[:, t, :], x[0, t * P:(t + 1) * P, :]).then_inc(x_first[t], 16)
            mlp(0, up0, down0)
            with turns(sp, HEADS) as h:
                s = ret0 + HEAD_SLICES * h
                w = ret_w_in[0]
                for u in range(4):
                    c0 = (u // 2) * qk_total + (u % 2) * P + h * 2 * P
                    load(s + u, columns(w, bass.ds(c0, P)), u)
                wk = w.rearrange("(k p) n -> p k n", p=P)
                for u in range(4):
                    load(s + 4 + u, (lambda r: r.rearrange("p (k n) -> p k n", k=2),
                                     wk[:, 2 * u:2 * u + 2, bass.ds(2 * qk_total + h * HV * P, HV * P)]), u)
                for u in range(4):
                    load(s + 8 + u, columns(w, bass.ds(2 * qk_total + v_total + h * HV * P + u * P, P)), u)
            down(ret_w_out[0], out0, VT)
            mlp(1, up1, down1)

        @block.gpsimd
        def _(pool):
            def row(ap):
                return ap.rearrange("(o n) -> o n", o=1).broadcast_to([P, d])

            pool.dma_start(gain_first[:, :], row(norm_gain[0, 0])).then_inc(pool_in, 16)
            pool.dma_start(pool_m[:, :], pool_tables).then_inc(pool_in, 16)
            pool.dma_start(small[:, :], small_tables).then_inc(pool_in, 16)
            pool.dma_start(pool_scale_b[:, :], row(pool_scale[0])).then_inc(pool_in, 16)
            pool.dma_start(pw_raw[:, :, :], pool_w[0].rearrange("g (c p) n -> p (g c) n", p=P)).then_inc(pool_in, 16)
            pool.dma_start(gain_post[:, :], row(norm_gain[0, 1])).then_inc(gain_in, 16)
            pool.dma_start(gain_pre[:, :], row(norm_gain[0, 2])).then_inc(gain_in, 16)
            for layer in range(2):
                pool.dma_start(par_rows[0:UP, 4 * layer:4 * layer + 3, :],
                               mlp_conv_w[layer].rearrange("a (t p) -> t a p", p=P)).then_inc(const_in, 16)
                pool.dma_start(par_rows[0:UP, 4 * layer + 3, :], mlp_conv_b[layer].rearrange("(t p) -> t p", p=P)).then_inc(const_in, 16)
            pool.dma_start(gn_rows[0:VT, :], ret_gn_gain[0].rearrange("(t p) -> t p", p=P)).then_inc(const_in, 16)

            def store(t, n, src, dst):
                pool.wait_ge(x1_done, n + 1)
                pool.dma_start(dst, src).then_inc(x_stored[t // TH] if n < LAST * TT else out_done, 16)

            for t in range(TT):
                store(t, t, x_p[:, t, :], x_scr[t])

            def residuals(sub, last_reader, half1_step):
                layer = sub // 2
                pool.wait_ge(slice_done, last_reader)
                if sub == 2:
                    pool.wait_ge(yt_stored, 16 * VT)
                else:
                    pool.wait_ge(mult_done, FT * (1 + layer))
                g_post = (1 if sub == 2 else 3)
                pool.dma_start(gain_post[:, :], row(norm_gain[layer, g_post])).then_inc(gain_in, 16)
                if sub < LAST:
                    pool.dma_start(gain_pre[:, :], row(norm_gain[1, 0 if sub == 1 else 2])).then_inc(gain_in, 16)
                for q in x_stored:
                    pool.wait_ge(q, 16 * TH * sub)
                for t in range(TH):
                    pool.dma_start(x_st0[:, t, :], x_scr[t]).then_inc(x_in[t], 16)
                for t in range(TH):
                    n = TT * sub + t
                    dst = x_scr[t] if sub < LAST else out[0, t * P:(t + 1) * P, :]
                    store(t, n, x_st0[:, t, :], dst)
                pool.wait_ge(gs_split, half1_step)
                for t in range(TH, TT):
                    pool.dma_start(x_st1[:, t - TH, :], x_scr[t]).then_inc(x_in[t], 16)
                if sub == 1:
                    pool.wait_ge(gs_split, 2 * FT)
                    pool.dma_start(pos_i[:, :], positions.broadcast_to([P, seq])).then_inc(pos_in, 16)
                for t in range(TH, TT):
                    n = TT * sub + t
                    dst = x_scr[t] if sub < LAST else out[0, t * P:(t + 1) * P, :]
                    store(t, n, x_st1[:, t - TH, :], dst)

            residuals(1, down0, FT + 12)

            chain = Tally(pool, pool_chain)
            pool.wait_ge(pos_in, 16)
            pool.wait_ge(pool_in, 80)
            ts, tt = pool.tensor_scalar, pool.tensor_tensor
            chain.mark(pool.tensor_copy(ang_a[:, :], pos_i[:, :]))
            chain.wait()
            chain.mark(ts(ang_a[:, :], ang_a[:, :], inv_freq, None, ALU.mult))
            chain.wait()
            for unit in (TURNS, 1.0):
                chain.mark(ts(ang_b[:, :], ang_a[:, :], 1.0 / (2.0 * np.pi * unit), ROUND, ALU.mult, ALU.add))
                chain.wait()
                chain.mark(ts(ang_b[:, :], ang_b[:, :], ROUND, None, ALU.subtract))
                chain.wait()
                for part in two_pi_parts():
                    chain.mark(ts(ang_c[:, :], ang_b[:, :], part * unit, None, ALU.mult))
                    chain.wait()
                    chain.mark(tt(ang_a[:, :], ang_a[:, :], ang_c[:, :], ALU.subtract))
                    chain.wait()
            chain.mark(ts(ang_b[:, :], ang_a[:, :], float(np.pi / 2), None, ALU.add))
            chain.wait()
            chain.mark(ts(ang_c[:, :], ang_b[:, :], float(np.pi), 2.0 * float(np.pi), ALU.is_gt, ALU.mult))
            chain.wait()
            chain.mark(tt(ang_b[:, :], ang_b[:, :], ang_c[:, :], ALU.subtract))
            chain.wait()
            pi32 = 3.1415925
            ts(ang_a[:, :], ang_a[:, :], pi32, -pi32, ALU.min, ALU.max).then_inc(ang_done, 1)
            ts(ang_b[:, :], ang_b[:, :], pi32, -pi32, ALU.min, ALU.max).then_inc(ang_done, 1)

            def store_head(h):
                for j in range(HV):
                    pool.wait_ge(yt_done, HV * h + HV + j + 1)
                    pool.dma_start(y_scr[bass.ds(HV * h + j, 1)].rearrange("o p n -> p (o n)") if h is not HEADS - 1
                                   else y_scr[HV * h + j], gate[:, j, :]).then_inc(yt_stored, 16)

            def bring_back(h):
                for j in range(HV):
                    f = HV * h + j
                    pool.dma_start(g_t[:, y_pos(f), :], y_scr[f]).then_inc(y_back[h], 16)

            pool.memset(flag_t[:, :], 0.0).then_inc(gate_free, 1)
            with turns(pool, HEADS - 1) as h:
                store_head(h)
                pool.wait_ge(yt_stored, 16 * HV * h + 16 * HV)
                pool.tensor_tensor(flag_t[:, :], flag_t[:, :], flag_t[:, :], ALU.add).then_inc(gate_free, 1)
            pool.wait_ge(slice_done, out0 - 3)
            pool.wait_ge(yt_stored, 16 * (HEADS - 1) * HV)
            for h in range(HEADS - 1):
                bring_back(h)
            store_head(HEADS - 1)
            pool.wait_ge(yt_stored, 16 * VT)
            bring_back(HEADS - 1)
            residuals(2, out0, 2 * FT + VT + 12)
            residuals(3, down1, 2 * FT + 2 * VT + FT + 12)
            pool.wait_ge(out_done, 16 * TT)
            for q in x_stored:
                pool.wait_ge(q, 16 * TH * LAST)

        @block.tensor
        def _(pe):
            mm = pe.matmul

            def three(dst, lhs, rhs, start, stop):
                mm(dst, lhs[0], rhs[0], start=start, stop=False)
                mm(dst, lhs[0], rhs[1], start=False, stop=False)
                return mm(dst, lhs[1], rhs[0], start=False, stop=stop)

            def w_cols(w, r, k):
                return w[:, r, k * P:(k + 1) * P]

            def project_half(r, bank, half):
                for k in range(KT):
                    last = three(ps[:, bank + half, :], (w_cols(w_hi, r, k), w_cols(w_lo, r, k)),
                                 (a_hi[:, half, k, :], a_lo[:, half, k, :]), k == 0, k == KT - 1)
                return last

            def project(s, r, bank):
                pe.wait_ge(w_split, s + 1)
                project_half(r, bank, 0)
                project_half(r, bank, 1).then_inc(slice_done, 1)

            def transposes(n, src, bank):
                pe.wait_ge(h_done, n + 1)
                for k in range(KT):
                    last = pe.transpose(pair(bank)[:, k * P:(k + 1) * P], src[:, k * P:(k + 1) * P], ident)
                last.then_inc(tr_done, 1)

            def pool_mix(t):
                pe.wait_ge(h0_done, t + 1)
                if t:
                    pe.wait_ge(d_split, t)
                for c in range(KT):
                    g = c // GC
                    dst = pair(0)[:, c * P:(c + 1) * P]
                    table = g if t == 0 else G + g
                    last = mm(dst, h0[:, t % 4, c * P:(c + 1) * P], pool_m[:, table * P:(table + 1) * P],
                              start=True, stop=(t == 0))
                    if t:
                        p0 = 2 * G * P + g * WMAX
                        last = mm(dst[:, 0:WMAX], h0[:, (t - 1) % 4, c * P:(c + 1) * P], pool_m[:, p0:p0 + WMAX],
                                  start=False, stop=True)
                last.then_inc(pool_done, 1)

            def pool_project(t):
                pe.wait_ge(d_split, t + 1)
                if t == 0:
                    pe.wait_ge(pw_split, 1)
                if t == 1:
                    pe.wait_ge(par_done, 2)
                if t >= 2:
                    pe.wait_ge(x1_done, t - 1)
                dst = pair(2 + 4 * (t % 2))
                for g in range(G):
                    for c in range(GC):
                        k = g * GC + c
                        last = three(dst[:, g * GW:(g + 1) * GW], (a_cols(a_hi, t)[:, k, :], a_cols(a_lo, t)[:, k, :]),
                                     (pw_hi[:, k, :], pw_lo[:, k, :]), c == 0, c == GC - 1)
                last.then_inc(y_done, 1)

            pe.wait_ge(const_in, 16 * 5)
            pe.wait_ge(pool_in, 80)
            for j in range(8):
                pe.transpose(ps[:, 7, j * UP:(j + 1) * UP], par_rows[0:UP, j, :], ident[0:UP, 0:UP])
            pe.transpose(ps[:, 7, 8 * UP:8 * UP + VT], gn_rows[0:VT, :], ident[0:VT, 0:VT]).then_inc(par_done, 1)

            for step in range(TT + 4):
                if 0 <= step - 1 < TT:
                    pool_mix(step - 1)
                if 0 <= step - 2 < TT:
                    pool_project(step - 2)
                t = step - 4
                if 0 <= t < TT:
                    if t >= 1:
                        pe.wait_ge(a_done, t)
                    transposes(t, y_stp[:, t % 4, :], 4)

            def up(sub, up_base):
                layer = sub // 2
                first_tile = UP * layer
                n0 = TT * sub
                for r in range(2):
                    pe.wait_ge(w_split, up_base + r + 1)
                    if r == 0:
                        pe.wait_ge(a_done, n0 - TH)
                    project_half(r, 2 * r, 0)
                if sub == LAST:
                    late_transposes(sub - 1)
                pe.wait_ge(a_done, n0)
                for r in range(2):
                    project_half(r, 2 * r, 1).then_inc(slice_done, 1)
                with turns(pe, FT - 1) as i:
                    for r in range(2):
                        pe.wait_ge(conv_done, first_tile + 2 * i + r + 1)
                        project(up_base + 2 * i + 2 + r, r, 2 * r)

            def down(down_base, nk, g_base, sub):
                def step(s, g, r, first, last, half):
                    pe.wait_ge(w_split, s + 1)
                    pe.wait_ge(gs_split, g + 1)
                    for t in range(TH):
                        if first and half == 1:
                            pe.wait_ge(drained_a, TH * 2 * (sub - 1) + t + 1)
                            pe.wait_ge(drained_v, TH * 2 * (sub - 1) + t + 1)
                        if first and half == 0 and t == 2 and sub != 2:
                            pe.wait_ge(conv_done, UP * (1 + sub // 2))
                        for n in range(2):
                            dst = ps[:, NEWEST[t] + n, :]
                            cols = slice(n * HALF, (n + 1) * HALF)
                            ins = three(dst, (gs_hi[:, r, t * P:(t + 1) * P], gs_lo[:, r, t * P:(t + 1) * P]),
                                        (w_hi[:, r, cols], w_lo[:, r, cols]), first, last)
                        if last and t < TH - 1:
                            ins.then_inc(y_done, 1)
                    ins.then_inc(slice_done, 1)

                for half in range(2):
                    s0, g0 = down_base + half * nk, g_base + half * nk
                    for k in range(2):
                        step(s0 + k, g0 + k, k, k == 0, False, half)
                    with turns(pe, (nk - 4) // 2) as i:
                        for u in range(2):
                            step(s0 + 2 + 2 * i + u, g0 + 2 + 2 * i + u, u, False, False, half)
                    for k in range(nk - 2, nk):
                        step(s0 + k, g0 + k, k % 2, False, k == nk - 1, half)
                if sub < LAST:
                    for t in range(TH):
                        pe.wait_ge(drained_a, TH * (2 * sub - 1) + t + 1)
                        pe.wait_ge(drained_v, TH * (2 * sub - 1) + t + 1)
                        transposes(TT * sub + t, y_st0[:, t, :], NEWEST[t])

            def late_transposes(sub):
                for t in range(TH, TT):
                    pe.wait_ge(a_done, TT * sub + t - 1)
                    transposes(TT * sub + t, y_st1[:, t - TH, :], NEWEST[t % 2])

            up(1, up0)
            down(down0, FT, 0, 1)
            late_transposes(1)

            def scores(h, m, half, j):
                lead = max(0, j - TH * half) * P
                if m >= 2:
                    pe.wait_ge(s_split, n_items * h + m - 1)
                dst = ps[:, 4 + m % 2, lead:HALF]
                for c in range(2):
                    jk, jc = j // TH, slice((j % TH) * P, (j % TH + 1) * P)
                    last = three(dst, (k_s[:, jk, 0, c, jc], k_s[:, jk, 1, c, jc]),
                                 (q_s[:, half, 0, c, lead:HALF], q_s[:, half, 1, c, lead:HALF]), c == 0, c == 1)
                last.then_inc(s_done, 1)

            def values(h, m, half, j):
                pe.wait_ge(s_split, n_items * h + m + 1)
                for i in range(max(j, TH * half), TH * half + TH):
                    if half == 1 and j == 0 and i >= TH + 2:
                        pe.wait_ge(o_copied, TT * h + i - TH - 1)
                    cols = slice((i - TH * half) * P, (i - TH * half + 1) * P)
                    dst = ps[:, (i if half == 0 else (i + 2) % 8), :]
                    last = three(dst, (s_hi[:, m % 2, cols], s_lo[:, m % 2, cols]),
                                 (v_hi[:, j, :], v_lo[:, j, :]), j == 0, j == i)
                    if i == j:
                        last.then_inc(o_done, 1)

            items = [(half, j) for half in range(2) for j in range(TH * half + TH)]
            n_items = len(items)
            pe.wait_ge(a_done, 2 * TT)
            with turns(pe, HEADS) as h:
                s = ret0 + HEAD_SLICES * h
                for u in range(4):
                    if u == 1:
                        pe.wait_ge(yt_done, HV * h + HV)
                    project(s + u, u % 2, 2 * u)
                for u in range(4):
                    pe.wait_ge(w_split, s + 4 + u + 1)
                    for t in range(TT):
                        if u == 0 and t in (0, 4, 6):
                            pe.wait_ge(rot_copied, 4 * h + {0: 2, 4: 3, 6: 4}[t])
                        for c in range(2):
                            k, r = 2 * u + c, u % 2
                            last = three(ps[:, t, :], (a_cols(a_hi, t)[:, k, :], a_cols(a_lo, t)[:, k, :]),
                                         (w_hi[:, r, c * HALF:(c + 1) * HALF], w_lo[:, r, c * HALF:(c + 1) * HALF]),
                                         k == 0, k == KT - 1)
                        if u == 3 and t < TT - 1:
                            last.then_inc(v_done, 1)
                    last.then_inc(slice_done, 1)
                pe.wait_ge(rot_split, 2 * h + 2)
                pe.wait_ge(v_split, TT * h + 6)
                scores(h, 0, *items[0])
                for m, (half, j) in enumerate(items):
                    if m + 1 < n_items:
                        scores(h, m + 1, *items[m + 1])
                    if (half, j) == (1, 0):
                        pe.wait_ge(v_split, TT * h + TT)
                    values(h, m, half, j)
                for j in range(HV):
                    if j == 0:
                        pe.wait_ge(o_copied, TT * h + TH)
                    if j >= 2:
                        pe.wait_ge(gate_done, HV * h + j - 1)
                    project(s + 8 + j, j % 2, 2 + 2 * (j % 2))
                pe.wait_ge(gn_done, TT * h + TT)
                for j in range(HV):
                    if j in (1, 2):
                        pe.wait_ge(gate_done, HV * h + j + 2)
                    if j == 3:
                        pe.wait_ge(yt_done, HV * h + HV + 1)
                    dst = pair((6, 2, 4, 6)[j])
                    for t in range(TT):
                        last = pe.transpose(dst[:, t * P:(t + 1) * P], o_s[:, t, j * P:(j + 1) * P], ident)
                    last.then_inc(ot_done, 1)
            pe.wait_ge(yt_done, HV * (HEADS + 1))
            down(out0, VT, 2 * FT, 2)
            up(3, up1)
            down(down1, FT, 2 * FT + 2 * VT, 3)

        @block.scalar
        def _(act):
            run = act.activation
            chain = Tally(act, act_chain)

            def split_w(s, slot):
                act.wait_ge(raw_full[slot], 16 * (s // 4 + 1))
                run(w_hi[:, slot % 2, :], w_raw[:, slot, :], ACT.Copy).then_inc(w_hi_done, 1)

            def split_loop(turn, first, u, after):
                act.wait_ge(slice_done, after)
                act.wait_ge(raw_full[(first + u) % 4], 16 * ((first + u) // 4 + 1) + 16 * turn)
                run(w_hi[:, (first + u) % 2, :], w_raw[:, (first + u) % 4, :], ACT.Copy).then_inc(w_hi_done, 1)

            def split_g(src, r):
                run(gs_hi[:, r, :], src, ACT.Copy).then_inc(gs_hi_done, 1)

            def root(n, src, col, done):
                t = n % TT
                chain.mark(run(junk[:, :], src, ACT.Square, accum_out=stat[:, t, col:col + 1]))
                chain.wait()
                run(stat[:, t, col + 1:col + 2], stat[:, t, col:col + 1], ACT.Sqrt,
                    scale=1.0 / d, bias=stat[:, 0, 7:8]).then_inc(done, 1)

            def norm_x(n, x_sb):
                act.wait_ge(x1_done, n + 1)
                root(n, x_sb, 3, x_root)

            def take_transposes(n, bank):
                act.wait_ge(tr_done, n + 1)
                run(a_cols(a_hi, n % TT), pair(bank).rearrange("p (k n) -> p k n", k=KT), ACT.Copy).then_inc(a_hi_done, 1)

            act.wait_ge(eps_done, 1)
            for t in range(TT + 4):
                if t < TT:
                    act.wait_ge(x_first[t], 16)
                    chain.mark(run(junk[:, :], x_p[:, t, :], ACT.Square, accum_out=stat[:, t, 0:1]))
                    chain.wait()
                    run(stat[:, t, 1:2], stat[:, t, 0:1], ACT.Sqrt, scale=1.0 / d, bias=stat[:, 0, 7:8]).then_inc(x0_root, 1)
                if t == 0:
                    act.wait_ge(pw_scaled, 1)
                    run(pw_hi[:, :, :], pw_raw[:, :, :], ACT.Copy).then_inc(pw_hi_done, 1)
                if t == 1:
                    split_w(0, 0)
                    split_w(1, 1)
                u = t - 1
                if 0 <= u < TT:
                    act.wait_ge(pool_done, u + 1)
                    run(a_cols(a_hi, u), pair(0).rearrange("p (k n) -> p k n", k=KT), ACT.Copy).then_inc(d_hi_done, 1)
                u = t - 2
                if 0 <= u < TT:
                    act.wait_ge(y_done, u + 1)
                    root(u, pair(2 + 4 * (u % 2)), 0, y_root)
                u = t - 3
                if 0 <= u < TT:
                    norm_x(u, x_p[:, u, :])
                u = t - 4
                if 0 <= u < TT:
                    take_transposes(u, 4)

            def up(sub, up_base):
                layer = sub // 2
                tile0, pair0 = UP * layer, FT * layer
                par = taps[:, layer, :, :]

                def body(turn, i, u2, slot_first, first):
                    s = up_base + 2 * i
                    for z in range(2):
                        split_loop(turn, slot_first, 2 * u2 + z, s + z + 1)
                        if z == 0 and not first:
                            act.wait_ge(mult_done, pair0 + i)
                        col = z * FT + i
                        run(conv[:, z, :], pair(2 * z), ACT.Identity,
                            scale=par[:, 2, bass.ds(col, 1)], bias=par[:, 3, bass.ds(col, 1)]).then_inc(tap_done, 1)
                        if z == 0:
                            act.wait_ge(conv_done, tile0 + 2 * i + 1)
                            run(conv[:, 0, :], conv[:, 0, :], ACT.Silu).then_inc(silu_done, 1)

                act.wait_ge(par_done, 2)
                for u2 in range(2):
                    body(0, u2, u2, up_base + 2, u2 == 0)
                with turns(act, FT // 2 - 1) as i:
                    for u2 in range(2):
                        body(i, 2 * i + 2 + u2, u2, up_base + 6, False)

            def down(down_base, nk, g_base, sub, g_src):
                layer = sub // 2
                if sub != 2:
                    act.wait_ge(mult_done, FT * (1 + layer))

                def split_ahead(s, slot_first, u, turn=0):
                    split_loop(turn, slot_first, u, s + 1)

                for half in range(2):
                    s0 = down_base + half * nk

                    def g_wait(k):
                        if sub == 2 and half == 0 and k % HV == 0:
                            act.wait_ge(y_back[k // HV], 16 * HV)

                    def g_split(k, r):
                        split_g(g_src(k, half), r)

                    if half == 0:
                        for k in range(2):
                            g_wait(k)
                            g_split(k, k)
                    straight, n_loop = plan_steps(nk, half, sub)
                    for k in range(straight):
                        split_ahead(s0 + k, s0 + k + 2, 0)
                        g_wait(k + 2)
                        g_split(k + 2, k % 2)
                        if half == 1:
                            first_half_norms(sub, k)
                    if n_loop:
                        with turns(act, n_loop) as i:
                            for u in range(4):
                                k = straight + 4 * i + u
                                split_ahead(s0 + k, s0 + straight + 2, u, i)
                                g_split(k + 2, (straight + u) % 2)
                    end = s0 + nk
                    if end < n_slices:
                        split_ahead(end - 2, end, 0)
                    if half == 0:
                        split_g(g_src(0, 1), 0)
                    stage = y_st0 if half == 0 else y_st1
                    for t in range(TH):
                        if t < TH - 1:
                            act.wait_ge(y_done, TT + (TH - 1) * (2 * (sub - 1) + half) + t + 1)
                        else:
                            act.wait_ge(slice_done, end)
                        run(stage[:, t, 0:HALF], ps[:, NEWEST[t], :], ACT.Copy).then_inc(drained_a, 1)
                    if end + 1 < n_slices:
                        split_ahead(end - 1, end + 1, 0)
                    if half == 0:
                        split_g(g_src(1, 1), 1)

                if sub < LAST:
                    for t in range(TH):
                        take_transposes(TT * sub + t, NEWEST[t])
                for step in range(TH + 2):
                    if step < TH:
                        n = TT * sub + TH + step
                        act.wait_ge(drained_v, TH * (2 * sub - 1) + step + 1)
                        act.wait_ge(drained_a, TH * (2 * sub - 1) + step + 1)
                        root(n, y_st1[:, step, :], 0, y_root)
                    if sub < LAST and 0 <= step - 1 < TH:
                        norm_x(TT * sub + TH + step - 1, x_st1[:, step - 1, :])
                    if sub < LAST and 0 <= step - 2 < TH:
                        take_transposes(TT * sub + TH + step - 2, NEWEST[(step - 2) % 2])

            def first_half_norms(sub, k):
                t = k // 2
                if t < TH:
                    n = TT * sub + t
                    if k % 2 == 0:
                        act.wait_ge(drained_v, TH * 2 * (sub - 1) + t + 1)
                        act.wait_ge(drained_a, TH * 2 * (sub - 1) + t + 1)
                        root(n, y_st0[:, t, :], 0, y_root)
                    elif sub < LAST:
                        norm_x(n, x_st0[:, t, :])

            up(1, up0)
            down(down0, FT, 0, 1, lambda k, half: (
                g_t[:, k, half * HALF:(half + 1) * HALF] if isinstance(k, int)
                else g_t[:, bass.ds(k, 1), half * HALF:(half + 1) * HALF].rearrange("p o n -> p (o n)")))

            act.wait_ge(ang_done, 2)
            run(sin_t[:, :], ang_a[:, :], ACT.Sin).then_inc(sin_done, 1)
            run(cos_t[:, :], ang_b[:, :], ACT.Sin).then_inc(sin_done, 1)
            items = [(half, j) for half in range(2) for j in range(TH * half + TH)]
            n_items = len(items)
            per_head = 0
            with turns(act, HEADS) as h:
                s = ret0 + HEAD_SLICES * h

                def ahead(u):
                    act.wait_ge(slice_done, s + u - 1)
                    act.wait_ge(raw_full[u % 4], 16 * ((ret0 + u) // 4 + 1) + 16 * (HEAD_SLICES // 4) * h)
                    run(w_hi[:, u % 2, :], w_raw[:, u % 4, :], ACT.Copy).then_inc(w_hi_done, 1)

                def high_parts(which, dst):
                    act.wait_ge(rot_f32, 2 * h + which + 1)
                    for c in range(2):
                        ins = run(dst[:, :, 0, c, :], rot[:, 2 + c, :].rearrange("p (b n) -> p b n", b=2), ACT.Copy)
                    ins.then_inc(rot_hi, 1)

                for u in range(4):
                    ahead(u + 2)
                    if u == 0:
                        act.wait_ge(gate_free, h + 1)
                    if u == 2:
                        high_parts(0, q_s)
                    run(rot[:, u % 2, :], pair(2 * u), ACT.Copy).then_inc(rot_copied, 1)
                ahead(6)
                high_parts(1, k_s)
                ahead(7)
                ahead(8)
                for t in range(TT):
                    if t < TT - 1:
                        act.wait_ge(v_done, (TT - 1) * h + t + 1)
                    else:
                        act.wait_ge(slice_done, s + 8)
                    run(v_hi[:, t, :], ps[:, t, :], ACT.Copy,
                        scale=v_decay[:, bass.ds(TT * h + t, 1)]).then_inc(v_hi_done, 1)
                ahead(9)

                def copy_out(i):
                    act.wait_ge(o_done, TT * h + i + 1)
                    run(o_s[:, i, :], ps[:, (i if i < TH else (i + 2) % 8), :], ACT.Copy,
                        scale=out_decay[:, bass.ds(TT * h + i, 1)]).then_inc(o_copied, 1)

                for m, (half, j) in enumerate(items):
                    lead = max(0, j - TH * half) * P
                    act.wait_ge(s_done, n_items * h + m + 1)
                    run(s_hi[:, m % 2, lead:HALF], ps[:, 4 + m % 2, lead:HALF], ACT.Copy).then_inc(s_hi_done, 1)
                    if m == TH:
                        copy_out(0)
                        copy_out(1)
                    if m == TH + 1:
                        copy_out(2)
                        copy_out(3)
                for i in range(TH, TT):
                    copy_out(i)
                for j in range(HV):
                    ahead(10 + j)
                    act.wait_ge(rot_split, 2 * h + 2)
                    run(gate[:, j, :], pair(2 + 2 * (j % 2)), ACT.Silu).then_inc(gate_done, 1)
                    if j == 0:
                        act.wait_ge(gn_var, h + 1)
                        run(gn_root[:, :], mv[:, :, 1], ACT.Sqrt, scale=1.0, bias=stat[:, 0, 7:8]).then_inc(gn_root_done, 1)
            act.wait_ge(yt_stored, 16 * VT)
            down(out0, VT, 2 * FT, 2, lambda k, half: (
                g_t[:, y_pos(k), half * HALF:(half + 1) * HALF] if isinstance(k, int)
                else g_t[:, bass.ds(y_pos(k), 1), half * HALF:(half + 1) * HALF].rearrange("p o n -> p (o n)")))
            up(3, up1)
            down(down1, FT, 2 * FT + 2 * VT, 3, lambda k, half: (
                g_t[:, k, half * HALF:(half + 1) * HALF] if isinstance(k, int)
                else g_t[:, bass.ds(k, 1), half * HALF:(half + 1) * HALF].rearrange("p o n -> p (o n)")))

        @block.vector
        def _(dve):
            chain = Tally(dve, dve_chain)
            tt, stt = dve.tensor_tensor, dve.scalar_tensor_tensor

            def split_w(s, slot):
                dve.wait_ge(w_hi_done, s + 1)
                tt(w_lo[:, slot % 2, :], w_raw[:, slot, :], f32(w_hi[:, slot % 2, :]), ALU.subtract).then_inc(w_split, 1)

            def split_g(g, src, r):
                dve.wait_ge(gs_hi_done, g + 1)
                tt(gs_lo[:, r, :], src, f32(gs_hi[:, r, :]), ALU.subtract).then_inc(gs_split, 1)

            def rstd(t, col):
                chain.mark(dve.reciprocal(stat[:, t, col + 2:col + 3], stat[:, t, col + 1:col + 2]))
                chain.wait()
                return stat[:, t, col + 2:col + 3]

            def norm_y(n, src, y_sb, x_sb, x_round):
                t = n % TT
                dve.wait_ge(y_root, n + 1)
                chain.mark(stt(out=y_sb, in0=src, scalar=rstd(t, 0), in1=gain_post[:, :], op0=ALU.mult, op1=ALU.mult))
                if x_round:
                    dve.wait_ge(x_in[t], 16 * x_round)
                chain.wait()
                tt(x_sb, x_sb, y_sb, ALU.add).then_inc(x1_done, 1)

            def norm_h(n, x_sb, y_sb):
                dve.wait_ge(x_root, n + 1)
                stt(out=y_sb, in0=x_sb, scalar=rstd(n % TT, 3), in1=gain_pre[:, :],
                    op0=ALU.mult, op1=ALU.mult).then_inc(h_done, 1)

            def take_transposes(n, bank):
                if n % TT >= TH and n >= TT:
                    dve.wait_ge(x_stored[0], 16 * TH * (n // TT + 1))
                dve.wait_ge(a_hi_done, n + 1)
                tt(a_cols(a_lo, n % TT), pair(bank).rearrange("p (k n) -> p k n", k=KT),
                   f32(a_cols(a_hi, n % TT)), ALU.subtract).then_inc(a_done, 1)

            dve.memset(stat[:, 0, 7:8], EPS).then_inc(eps_done, 1)
            dve.wait_ge(pool_in, 80)
            for t in range(TT + 4):
                if t < TT:
                    dve.wait_ge(x0_root, t + 1)
                    if t >= 4:
                        dve.wait_ge(pool_done, t - 2)
                    stt(out=h0[:, t % 4, :], in0=x_p[:, t, :], scalar=rstd(t, 0), in1=gain_first[:, :],
                        op0=ALU.mult, op1=ALU.mult).then_inc(h0_done, 1)
                if t == 0:
                    w4 = pw_raw[:, :, :].rearrange("p (g c) n -> p g c n", g=G)
                    s3 = pool_scale_b[:, :].rearrange("p (g n) -> p g n", g=G)
                    for c in range(GC):
                        ins = tt(w4[:, :, c, :], w4[:, :, c, :], s3, ALU.mult)
                    ins.then_inc(pw_scaled, 1)
                    dve.wait_ge(pw_hi_done, 1)
                    tt(pw_lo[:, :, :], pw_raw[:, :, :], f32(pw_hi[:, :, :]), ALU.subtract).then_inc(pw_split, 1)
                if t == 1:
                    dve.wait_ge(par_done, 1)
                    dve.tensor_copy(taps[:, :, :, :].rearrange("p l a t -> p (l a t)"), ps[:, 7, 0:8 * UP])
                    dve.tensor_copy(gn_gain[:, :], ps[:, 7, 8 * UP:8 * UP + VT]).then_inc(par_done, 1)
                    split_w(0, 0)
                    split_w(1, 1)
                u = t - 1
                if 0 <= u < TT:
                    dve.wait_ge(d_hi_done, u + 1)
                    tt(a_cols(a_lo, u), pair(0).rearrange("p (k n) -> p k n", k=KT), f32(a_cols(a_hi, u)),
                       ALU.subtract).then_inc(d_split, 1)
                u = t - 2
                if 0 <= u < TT:
                    if u == 0:
                        dve.wait_ge(gain_in, 32)
                    if u >= 4:
                        dve.wait_ge(tr_done, u - 3)
                    norm_y(u, pair(2 + 4 * (u % 2)), y_stp[:, u % 4, :], x_p[:, u, :], 0)
                u = t - 3
                if 0 <= u < TT:
                    norm_h(u, x_p[:, u, :], y_stp[:, u % 4, :])
                u = t - 4
                if 0 <= u < TT:
                    take_transposes(u, 4)

            def up(sub, up_base):
                layer = sub // 2
                tile0, pair0 = UP * layer, FT * layer
                par = taps[:, layer, :, :]
                for q in x_stored:
                    dve.wait_ge(q, 16 * TH * sub)
                with turns(dve, FT // 2, chain, 4) as turn:
                    for u2 in range(2):
                        i = 2 * turn + u2
                        for z in range(2):
                            split_w(up_base + 2 * i + z + 2, (up_base + 2 * u2 + z + 2) % 4)
                            tile = tile0 + 2 * i + z
                            dve.wait_ge(tap_done, tile + 1)
                            col = z * FT + i
                            for back in (1, 2):
                                ins = stt(out=conv[:, z, back:], in0=pair(2 * z)[:, 0:seq - back],
                                          scalar=par[:, 2 - back, bass.ds(col, 1)], in1=conv[:, z, back:],
                                          op0=ALU.mult, op1=ALU.add)
                                if back == 1:
                                    chain.mark(ins)
                                    chain.wait()
                            ins.then_inc(conv_done, 1)
                        dve.wait_ge(silu_done, pair0 + i + 1)
                        dve.wait_ge(conv_done, tile0 + 2 * i + 2)
                        tt(g_t[:, bass.ds(i, 1), :].rearrange("p o n -> p (o n)"), conv[:, 0, :], conv[:, 1, :],
                           ALU.mult).then_inc(mult_done, 1)

            def down(down_base, nk, g_base, sub, g_src):
                for half in range(2):
                    s0, g0 = down_base + half * nk, g_base + half * nk
                    if half == 0:
                        for k in range(2):
                            split_g(g0 + k, g_src(k, 0), k)
                    straight, n_loop = plan_steps(nk, half, sub)
                    for k in range(straight):
                        split_w(s0 + k + 2, (s0 + k + 2) % 4)
                        split_g(g0 + k + 2, g_src(k + 2, half), k % 2)
                        if half == 1:
                            first_half_norms(sub, k)
                    if n_loop:
                        with turns(dve, n_loop) as i:
                            for u in range(4):
                                k = straight + 4 * i + u
                                split_w(s0 + k + 2, (s0 + straight + 2 + u) % 4)
                                split_g(g0 + k + 2, g_src(k + 2, half), (straight + u) % 2)
                    end = s0 + nk
                    if end < n_slices:
                        split_w(end, end % 4)
                    if half == 0:
                        split_g(g0 + nk, g_src(0, 1), 0)
                    stage = y_st0 if half == 0 else y_st1
                    for t in range(TH):
                        if t < TH - 1:
                            dve.wait_ge(y_done, TT + (TH - 1) * (2 * (sub - 1) + half) + t + 1)
                        else:
                            dve.wait_ge(slice_done, end)
                        dve.tensor_copy(stage[:, t, HALF:d], ps[:, NEWEST[t] + 1, :]).then_inc(drained_v, 1)
                    if end + 1 < n_slices:
                        split_w(end + 1, (end + 1) % 4)
                    if half == 0:
                        split_g(g0 + nk + 1, g_src(1, 1), 1)

                if sub < LAST:
                    for t in range(TH):
                        take_transposes(TT * sub + t, NEWEST[t])
                for step in range(TH + 2):
                    if step < TH:
                        norm_y(TT * sub + TH + step, y_st1[:, step, :], y_st1[:, step, :], x_st1[:, step, :], sub)
                    if sub < LAST and 0 <= step - 1 < TH:
                        norm_h(TT * sub + TH + step - 1, x_st1[:, step - 1, :], y_st1[:, step - 1, :])
                    if sub < LAST and 0 <= step - 2 < TH:
                        take_transposes(TT * sub + TH + step - 2, NEWEST[(step - 2) % 2])

            def first_half_norms(sub, k):
                t = k // 2
                if t < TH:
                    n = TT * sub + t
                    if k == 0:
                        dve.wait_ge(gain_in, 32 * (sub + 1) if sub < LAST else 32 * sub + 16)
                    if k % 2 == 0:
                        norm_y(n, y_st0[:, t, :], y_st0[:, t, :], x_st0[:, t, :], sub)
                    elif sub < LAST:
                        norm_h(n, x_st0[:, t, :], y_st0[:, t, :])

            def hidden(k, half):
                cols = slice(half * HALF, (half + 1) * HALF)
                if isinstance(k, int):
                    return g_t[:, k, cols]
                return g_t[:, bass.ds(k, 1), cols].rearrange("p o n -> p (o n)")

            def heads_out(k, half):
                return hidden(y_pos(k), half)

            up(1, up0)
            down(down0, FT, 0, 1, hidden)

            items = [(half, j) for half in range(2) for j in range(TH * half + TH)]
            n_items = len(items)
            for q in x_stored:
                dve.wait_ge(q, 16 * TH * 2)
            dve.memset(stat[:, 1, 7:8], 0.0).then_inc(yt_done, HV)
            dve.wait_ge(sin_done, 2)
            n_diag = TT
            with turns(dve, HEADS, chain, 2 * 5 + n_diag + TT + 1) as h:
                s = ret0 + HEAD_SLICES * h

                def ahead(u):
                    split_w(s + u, u % 4)

                def rotate(which):
                    dve.wait_ge(rot_copied, 4 * h + 2 * which + 2)
                    if which:
                        dve.wait_ge(rot_split, 2 * h + 1)
                    chain.mark(tt(rot[:, 2, :], rot[:, 0, :], cos_t[:, :], ALU.mult))
                    chain.mark(tt(rot[:, 3, :], rot[:, 1, :], cos_t[:, :], ALU.mult))
                    chain.wait(1)
                    chain.mark(tt(rot[:, 0, :], rot[:, 0, :], sin_t[:, :], ALU.mult))
                    chain.wait(1)
                    chain.mark(tt(rot[:, 1, :], rot[:, 1, :], sin_t[:, :], ALU.mult))
                    chain.wait(1)
                    chain.mark(tt(rot[:, 3, :], rot[:, 3, :], rot[:, 0, :], ALU.add))
                    chain.wait(1)
                    tt(rot[:, 2, :], rot[:, 2, :], rot[:, 1, :], ALU.subtract).then_inc(rot_f32, 1)

                def low_parts(which, dst):
                    dve.wait_ge(rot_hi, 2 * h + which + 1)
                    for c in range(2):
                        ins = tt(dst[:, :, 1, c, :], rot[:, 2 + c, :].rearrange("p (b n) -> p b n", b=2),
                                 f32(dst[:, :, 0, c, :]), ALU.subtract)
                    ins.then_inc(rot_split, 1)

                ahead(2)
                ahead(3)
                rotate(0)
                ahead(4)
                low_parts(0, q_s)
                ahead(5)
                rotate(1)
                ahead(6)
                low_parts(1, k_s)
                ahead(7)
                ahead(8)
                for t in range(TT):
                    dve.wait_ge(v_hi_done, TT * h + t + 1)
                    stt(out=v_lo[:, t, :], in0=ps[:, t, :], scalar=v_decay[:, bass.ds(TT * h + t, 1)],
                        in1=f32(v_hi[:, t, :]), op0=ALU.mult, op1=ALU.subtract).then_inc(v_split, 1)
                ahead(9)
                for m, (half, j) in enumerate(items):
                    lead = max(0, j - TH * half) * P
                    r = m % 2
                    dve.wait_ge(s_hi_done, n_items * h + m + 1)
                    ins = tt(s_lo[:, r, lead:HALF], ps[:, 4 + r, lead:HALF], f32(s_hi[:, r, lead:HALF]), ALU.subtract)
                    if j >= TH * half:
                        chain.mark(ins)
                        chain.wait()
                        diag = slice(lead, lead + P)
                        tt(s_hi[:, r, diag], f32(s_hi[:, r, diag]), causal, ALU.mult)
                        ins = tt(s_lo[:, r, diag], f32(s_lo[:, r, diag]), causal, ALU.mult)
                    ins.then_inc(s_split, 1)
                for i in range(TT):
                    dve.wait_ge(o_copied, TT * h + i + 1)
                    chain.mark(dve.bn_stats(bn6[:, i, :], o_s[:, i, :]))
                chain.wait()
                dve.memset(stat[:, 1, 7:8], 0.0)
                for i in range(TT):
                    ins = dve.bn_aggr(mv[:, i, :], bn6[:, i, :])
                ins.then_inc(gn_var, 1)
                ahead(10)
                dve.wait_ge(gn_root_done, h + 1)
                chain.mark(dve.reciprocal(gn_rstd[:, :], gn_root[:, :]))
                chain.wait()
                for i in range(TT):
                    dve.tensor_scalar(o_s[:, i, :], o_s[:, i, :], mv[:, i, 0:1], gn_rstd[:, i:i + 1],
                                      ALU.subtract, ALU.mult).then_inc(gn_done, 1)
                ahead(11)
                ahead(12)
                ahead(13)
                for j in range(HV):
                    dve.wait_ge(ot_done, HV * h + j + 1)
                    dve.wait_ge(gate_done, HV * h + j + 1)
                    stt(out=gate[:, j, :], in0=pair((6, 2, 4, 6)[j]), scalar=gn_gain[:, bass.ds(HV * h + j, 1)],
                        in1=gate[:, j, :], op0=ALU.mult, op1=ALU.mult).then_inc(yt_done, 1)
            down(out0, VT, 2 * FT, 2, heads_out)
            up(3, up1)
            down(down1, FT, 2 * FT + 2 * VT, 3, hidden)


_OUT = ((1, 1024, 1024), "float32")


def kernel(**inputs):
    import concourse.bacc as bacc
    from concourse.bass_utils import run_bass_kernel_spmd

    nc = bacc.Bacc("TRN2", target_bir_lowering=False, num_devices=1)
    pool_tables, small_tables = shape_constants(inputs["x"].shape[1])
    named = dict(inputs)
    named["pool_tables"], named["small_tables"] = pool_tables, small_tables
    arrays, args = {}, {}
    for name, a in named.items():
        a = np.ascontiguousarray(a)
        arrays[f"in_{name}"] = a
        args[name] = nc.dram_tensor(f"in_{name}", a.shape, mybir.dt.from_np(a.dtype), kind="ExternalInput").ap()
    args["out"] = nc.dram_tensor("out_x", _OUT[0], F32, kind="ExternalOutput").ap()
    hybrid_trunk(nc, **args)
    r = run_bass_kernel_spmd(nc, [arrays], core_ids=[0])
    return r.results[0]["out_x"]
```

```python
from contextlib import ExitStack, contextmanager

import concourse.bass as bass
from concourse import mybir
import numpy as np

ALU = mybir.AluOpType
ACT = mybir.ActivationFunctionType
F32 = mybir.dt.float32
F32R = mybir.dt.float32r
BF16 = mybir.dt.bfloat16
I32 = mybir.dt.int32

P = 128
HALF = 512
WINDOWS = (2, 4, 8, 16)
HEADS = 4
CHUNKS_UP = 4
EPS = 1e-6
ROUND = 12582912.0
TURNS = 4096.0


def two_pi_parts():
    rest, parts = 2.0 * np.pi, []
    for _ in range(2):
        scale = 2.0 ** (11 - np.floor(np.log2(abs(rest))))
        part = np.round(rest * scale) / scale
        parts.append(float(part))
        rest -= part
    return parts + [float(np.float32(rest))]


def shape_constants(seq):
    s, t = np.arange(P)[:, None], np.arange(P)[None, :]
    first, main, prev = [], [], []
    for win in WINDOWS:
        inside = (s <= t) & (s > t - win)
        count = np.minimum(t + 1, win)
        first.append(inside / count - (s == t))
        main.append(inside / win - (s == t))
        w = np.arange(max(WINDOWS))[None, :]
        prev.append((s - P > w - win) / win)
    pool = np.concatenate(main + prev + first, axis=1).astype(np.float32)
    log_gamma = np.log(1.0 - 2.0 ** (-5.0 - np.arange(HEADS)))
    tok = np.arange(seq).reshape(-1, P).T
    qk_dim = 2 * P
    out_decay = np.exp(tok[:, None, :] * log_gamma[None, :, None]) * qk_dim ** -0.5
    v_decay = np.exp(-tok[:, None, :] * log_gamma[None, :, None])
    inv_freq = 10000.0 ** (-np.arange(P) / P)
    small = np.concatenate([
        np.eye(P), (s <= t),
        out_decay.reshape(P, -1), v_decay.reshape(P, -1), inv_freq[:, None],
    ], axis=1).astype(np.float32)
    return pool, small


class Tally:

    def __init__(self, eng, sem):
        self.eng, self.sem, self.base, self.local = eng, sem, 0, 0

    def mark(self, ins):
        ins.then_inc(self.sem, 1)
        self.local += 1

    def wait(self, but=0):
        self.eng.wait_ge(self.sem, self.base + self.local - but)


@contextmanager
def turns(eng, count, tally=None, per_turn=0):
    before = tally.base + tally.local if tally else 0
    with eng.Fori(0, count) as i:
        if tally:
            tally.base, tally.local = before + i * per_turn, 0
        yield i
        if tally:
            assert tally.local == per_turn, (tally.local, per_turn)
    if tally:
        tally.base, tally.local = before + count * per_turn, 0


def hybrid_trunk(nc, x, positions, norm_gain, pool_w, pool_scale, ret_w_in, ret_gn_gain, ret_w_out,
                 mlp_w_up, mlp_conv_w, mlp_conv_b, mlp_w_down, pool_tables, small_tables, out):
    seq, d = x.shape[1], x.shape[2]
    KT = d // P
    TT = seq // P
    TH = TT // 2
    dff = mlp_w_down.shape[1]
    FT = dff // P
    VT = ret_w_out.shape[1] // P
    HV = VT // HEADS
    G = len(WINDOWS)
    GC = KT // G
    GW = d // G
    WMAX = max(WINDOWS)
    qk_total = HEADS * 2 * P
    v_total = VT * P
    assert (seq, d, KT, TT) == (2 * HALF, 1024, 8, 8) and FT % 2 == 0

    UP = 2 * FT
    HEAD_SLICES = 12
    up0, down0 = 0, UP
    ret0 = down0 + 2 * FT
    out0 = ret0 + HEADS * HEAD_SLICES
    up1 = out0 + 2 * VT
    down1 = up1 + UP
    n_slices = down1 + 2 * FT

    ctx = ExitStack()
    with ctx:
        base = (nc.sbuf_base + 31) // 32 * 32
        arena = nc.sbuf_usable_end - base
        KB = 1024
        off = {}
        at = base
        for name, size in (("A", 64 * KB), ("G", 88 * KB), ("raw", 16 * KB), ("w", 16 * KB), ("T", 16 * KB)):
            off[name] = at
            at += size

        def place(name, shape, dt, region, byte=0):
            return nc.alloc_sbuf_tensor_at(name, shape, dt, offset=off[region] + byte)

        TILE = 4 * KB
        a_hi = place("a_hi", [P, 2, KT, HALF], F32R, "A")
        a_lo = place("a_lo", [P, 2, KT, HALF], F32R, "A", 32 * KB)
        y_st0 = place("y_st0", [P, TH, d], F32, "A", 16 * KB)
        x_st0 = place("x_st0", [P, TH, d], F32, "A", 48 * KB)
        g_t = place("g_t", [P, FT, seq], F32, "G")
        y_st1 = place("y_st1", [P, TH, d], F32, "G")
        x_st1 = place("x_st1", [P, TH, d], F32, "G", 8 * TILE)
        x_p = place("x_p", [P, TT, d], F32, "G")
        MIX = G * (P + WMAX)
        mix = place("mix", [P, 4, MIX], F32, "G", 8 * TILE)
        y_stp = place("y_stp", [P, 4, d], F32, "G", 12 * TILE)
        pw_raw = place("pw_raw", [P, KT, GW], F32, "G", 12 * TILE)
        pw_hi = place("pw_hi", [P, KT, GW], F32R, "G", 16 * TILE)
        pw_lo = place("pw_lo", [P, KT, GW], F32R, "G", 18 * TILE)
        par_rows = place("par_rows", [P, 8, P], F32, "G", 14 * TILE)
        gn_rows = place("gn_rows", [P, P], F32, "G", 15 * TILE)
        gain_rows = place("gain_rows", [P, P], F32, "G", 15 * TILE + 512)
        gain_first = place("gain_first", [P, KT], F32, "G", 20 * TILE)
        pool_scale_b = place("pool_scale_b", [P, d], F32, "G", 21 * TILE)
        q_s = place("q_s", [P, 2, 2, 2, HALF], F32R, "G")
        o_s = place("o_s", [P, TT, HALF], F32, "G")
        k_s = place("k_s", [P, 2, 2, 2, HALF], F32R, "G", 4 * TILE)
        v_hi = place("v_hi", [P, TT, HALF], F32R, "G", 8 * TILE)
        v_lo = place("v_lo", [P, TT, HALF], F32R, "G", 12 * TILE)
        s_hi = place("s_hi", [P, 2, HALF], F32R, "G", 16 * TILE)
        s_lo = place("s_lo", [P, 2, HALF], F32R, "G", 17 * TILE)
        cos_t = place("cos_t", [P, seq], F32, "G", 20 * TILE)
        sin_t = place("sin_t", [P, seq], F32, "G", 21 * TILE)
        gs_hi_r = place("gs_hi_r", [P, 2, HALF], F32R, "G", 20 * TILE)
        gs_lo_r = place("gs_lo_r", [P, 2, HALF], F32R, "G", 21 * TILE)
        w_raw = place("w_raw", [P, 4, d], F32, "raw")
        w_hi = place("w_hi", [P, 2, d], F32R, "w")
        w_lo = place("w_lo", [P, 2, d], F32R, "w", 8 * KB)
        conv = place("conv", [P, 2, seq], F32, "T")
        junk = place("junk", [P, d], BF16, "T")
        gain_post = place("gain_post", [P, d], F32, "T", 4 * KB)
        gs_hi = place("gs_hi", [P, 2, HALF], F32R, "T", 8 * KB)
        gs_lo = place("gs_lo", [P, 2, HALF], F32R, "T", 12 * KB)
        mix_m = place("mix_m", [P, pool_tables.shape[1]], F32, "T", 8 * KB)
        rot = place("rot", [P, 4, seq], F32, "T")
        gate = place("gate", [P, HV, seq], F32, "T")
        off["C"] = at
        gain_pre = place("gain_pre", [P, d], F32, "C")
        AW = seq // 4
        ang_a = place("ang_a", [P, AW], F32, "C")
        ang_b = place("ang_b", [P, AW], F32, "C", 4 * AW)
        ang_c = place("ang_c", [P, AW], F32, "C", 8 * AW)
        pos_i = place("pos_i", [P, AW], I32, "C", 12 * AW)
        small = place("small", [P, small_tables.shape[1]], F32, "C", 4 * KB)
        at += 4 * KB + (small_tables.shape[1] * 4 + 31) // 32 * 32
        off["D"] = at
        taps = place("taps", [P, 2, 4, UP], F32, "D")
        at += 2 * 4 * UP * 4
        off["E"] = at
        gn_gain = place("gn_gain", [P, VT], F32, "E")
        stat = place("stat", [P, TT, 8], F32, "E", 64)
        bn6 = place("bn6", [P, TT, 6], F32, "E", 64 + 256)
        mv = place("mv", [P, TT, 2], F32, "E", 64 + 256 + 192)
        gn_root = place("gn_root", [P, TT], F32, "E", 64 + 256 + 192 + 64)
        gn_rstd = place("gn_rstd", [P, TT], F32, "E", 64 + 256 + 192 + 96)
        flag_t = place("flag_t", [P, 1], F32, "E", 64 + 256 + 192 + 128)
        assert at + 64 + 256 + 192 + 160 <= base + arena, (at, base, arena)

        ident = small[:, 0:P]
        causal = small[:, P:2 * P]
        nd = HEADS * TT
        out_decay = small[:, 2 * P:2 * P + nd]
        v_decay = small[:, 2 * P + nd:2 * P + 2 * nd]
        inv_freq = small[:, 2 * P + 2 * nd:2 * P + 2 * nd + 1]

        ps = ctx.enter_context(nc.psum_tensor("ps", [P, 8, HALF], F32))

        def pair(b):
            return ps[:, b:b + 2, :].rearrange("p b n -> p (b n)")

        x_scr = nc.dram_tensor("x_scratch", (TT, P, d), F32).ap()
        ang_scr = nc.dram_tensor("angle_scratch", (2, P, seq), F32).ap()
        y_scr = nc.dram_tensor("y_scratch", (VT, P, seq), F32).ap()

        def sem(name):
            return ctx.enter_context(nc.semaphore(name))

        raw_full = [sem(f"raw_full{j}") for j in range(4)]
        w_hi_done, w_split = sem("w_hi_done"), sem("w_split")
        slice_done = sem("slice_done")
        tap_done, conv_done, silu_done, mult_done = (sem(n) for n in ("tap_done", "conv_done", "silu_done", "mult_done"))
        gs_hi_done, gs_split = sem("gs_hi_done"), sem("gs_split")
        y_done, drained_a, drained_v = sem("y_done"), sem("drained_a"), sem("drained_v")
        y_root, yn_done, x1_done, x_root, h_done = (sem(n) for n in ("y_root", "yn_done", "x1_done", "x_root", "h_done"))
        tr_done, a_hi_done, a_done = sem("tr_done"), sem("a_hi_done"), sem("a_done")
        x_first = [sem(f"x_first{t}") for t in range(TT)]
        x_in = [sem(f"x_in{t}") for t in range(TT)]
        x_stored = [sem("x_stored0"), sem("x_stored1")]
        gain_in, const_in, par_done, eps_done = sem("gain_in"), sem("const_in"), sem("par_done"), sem("eps_done")
        small_in, mix_in, rows_in, scale_in, taps_out = (
            sem(n) for n in ("small_in", "mix_in", "rows_in", "scale_in", "taps_out"))
        x0_root, mix_scaled, pool_done, d_hi_done, d_split = (
            sem(n) for n in ("x0_root", "mix_scaled", "pool_done", "d_hi_done", "d_split"))
        pw_scaled, pw_hi_done, pw_split, pw_in = (sem(n) for n in ("pw_scaled", "pw_hi_done", "pw_split", "pw_in"))
        pos_in, ang_done, ang_stored, ang_in, sin_done = (
            sem(n) for n in ("pos_in", "ang_done", "ang_stored", "ang_in", "sin_done"))
        rot_copied, rot_f32, rot_hi, rot_split = (sem(n) for n in ("rot_copied", "rot_f32", "rot_hi", "rot_split"))
        v_done, v_hi_done, v_split = sem("v_done"), sem("v_hi_done"), sem("v_split")
        s_done, s_hi_done, s_split = sem("s_done"), sem("s_hi_done"), sem("s_split")
        o_done, o_copied = sem("o_done"), sem("o_copied")
        gate_done, gn_var, gn_root_done, gn_done = (sem(n) for n in ("gate_done", "gn_var", "gn_root_done", "gn_done"))
        ot_done, yt_done, yt_stored, gate_free = (sem(n) for n in ("ot_done", "yt_done", "yt_stored", "gate_free"))
        y_back = [sem(f"y_back{h}") for h in range(HEADS)]
        out_done = sem("out_done")
        act_chain, dve_chain, pool_chain = sem("act_chain"), sem("dve_chain"), sem("pool_chain")

        LAST = 3

        def bank_of(sub, half, t):
            if half:
                return 2 * t
            return ((0, 4, 6, 2) if sub == 2 else (4, 6, 0, 2))[t]

        def late_bank(t):
            return (4, 6)[t % 2]

        def plan_steps(nk, half, sub):
            lead = 2 * TH if half == 1 else (nk - 2 if sub == 2 else 0)
            n_loop = (nk - 2 - lead) // 4
            return nk - 2 - 4 * n_loop, n_loop

        def pool_adds(n):
            return n < LAST * TT + TH

        def y_pos(f):
            return VT + 3 - f

        def hidden(k, half):
            cols = slice(half * HALF, (half + 1) * HALF)
            if isinstance(k, int):
                return g_t[:, k, cols]
            return g_t[:, bass.ds(k, 1), cols].rearrange("p o n -> p (o n)")

        def heads_out(k, half):
            return hidden(y_pos(k), half)

        def a_cols(a, t):
            return a[:, t // TH, :, (t % TH) * P:(t % TH + 1) * P]

        def f32(ap):
            return ap.bitcast(F32)

        block = ctx.enter_context(nc.Block())

        @block.sync
        def _(sp):
            def load(s, src, slot, first=False):
                if not first:
                    sp.wait_ge(w_split, s - 3)
                sp.dma_start(src[0](w_raw[:, slot, :]), src[1]).then_inc(raw_full[slot], 16)

            def flat(ap):
                return ap

            def columns(w, c0):
                return (lambda r: r.rearrange("p (k n) -> p k n", k=KT),
                        w.rearrange("(k p) n -> p k n", p=P)[:, :, c0])

            def up_load(layer, i, z, s, slot, first=False):
                load(s, columns(mlp_w_up[layer], bass.ds(z * dff + i * P, P)), slot, first)

            def mlp(layer, up_base, down_base):
                def four(i0, s0, first=False):
                    for u in range(4):
                        up_load(layer, i0 + u // 2, u % 2, s0 + u, u, first)
                if up_base == 0:
                    four(0, 0, True)
                    with turns(sp, FT // 2 - 1) as i:
                        four(2 * i + 2, 4 * i + 4)
                else:
                    with turns(sp, FT // 2) as i:
                        four(2 * i, 4 * i + up_base)
                down(mlp_w_down[layer], down_base, FT)

            def down(w, down_base, nk):
                rows = w.rearrange("(k p) n -> k p n", p=P)
                for half in range(2):
                    s0 = down_base + half * nk
                    lead = nk % 4
                    for k in range(lead):
                        load(s0 + k, (flat, rows[k]), (s0 + k) % 4)
                    with turns(sp, nk // 4) as i:
                        for u in range(4):
                            src = rows[bass.ds(lead + 4 * i + u, 1)].rearrange("o p n -> p (o n)")
                            load(s0 + lead + 4 * i + u, (flat, src), (s0 + lead + u) % 4)

            for t in range(TT):
                sp.dma_start(x_p[:, t, :], x[0, t * P:(t + 1) * P, :]).then_inc(x_first[t], 16)
            mlp(0, up0, down0)
            with turns(sp, HEADS) as h:
                s = ret0 + HEAD_SLICES * h
                w = ret_w_in[0]
                for u in range(4):
                    c0 = (u // 2) * qk_total + (u % 2) * P + h * 2 * P
                    load(s + u, columns(w, bass.ds(c0, P)), u)
                wk = w.rearrange("(k p) n -> p k n", p=P)
                for u in range(4):
                    load(s + 4 + u, (lambda r: r.rearrange("p (k n) -> p k n", k=2),
                                     wk[:, 2 * u:2 * u + 2, bass.ds(2 * qk_total + h * HV * P, HV * P)]), u)
                for u in range(4):
                    load(s + 8 + u, columns(w, bass.ds(2 * qk_total + v_total + h * HV * P + u * P, P)), u)
            down(ret_w_out[0], out0, VT)
            mlp(1, up1, down1)

        @block.gpsimd
        def _(pool):
            def row(ap):
                return ap.rearrange("(o n) -> o n", o=1).broadcast_to([P, d])

            pool.dma_start(gain_rows[0:KT, :], norm_gain[0, 0].rearrange("(t p) -> t p", p=P)).then_inc(rows_in, 16)
            pool.dma_start(pool_scale_b[:, :], row(pool_scale[0])).then_inc(scale_in, 16)
            pool.dma_start(gain_post[:, :], row(norm_gain[0, 1])).then_inc(gain_in, 16)
            pool.dma_start(gain_pre[:, :], row(norm_gain[0, 2])).then_inc(gain_in, 16)
            for layer in range(2):
                pool.dma_start(par_rows[0:UP, 4 * layer:4 * layer + 3, :],
                               mlp_conv_w[layer].rearrange("a (t p) -> t a p", p=P)).then_inc(const_in, 16)
                pool.dma_start(par_rows[0:UP, 4 * layer + 3, :], mlp_conv_b[layer].rearrange("(t p) -> t p", p=P)).then_inc(const_in, 16)
            pool.dma_start(gn_rows[0:VT, :], ret_gn_gain[0].rearrange("(t p) -> t p", p=P)).then_inc(const_in, 16)

            def add_and_store(t, n, x_sb, y_sb, dst):
                if pool_adds(n):
                    pool.wait_ge(yn_done, n + 1)
                    if n >= TT:
                        pool.wait_ge(x_in[t], 16 * (n // TT))
                    pool.tensor_tensor(x_sb, x_sb, y_sb, ALU.add).then_inc(x1_done, 1)
                pool.wait_ge(x1_done, n + 1)
                pool.dma_start(dst, x_sb).then_inc(x_stored[t // TH] if n < LAST * TT else out_done, 16)

            for t in range(TT):
                add_and_store(t, t, x_p[:, t, :], y_stp[:, t % 4, :], x_scr[t])

            def residuals(sub, last_reader, half1_step):
                layer = sub // 2
                pool.wait_ge(slice_done, last_reader)
                if sub == 2:
                    pool.wait_ge(yt_stored, 16 * VT)
                else:
                    pool.wait_ge(mult_done, FT * (1 + layer))
                g_post = (1 if sub == 2 else 3)
                pool.dma_start(gain_post[:, :], row(norm_gain[layer, g_post])).then_inc(gain_in, 16)
                if sub < LAST:
                    pool.dma_start(gain_pre[:, :], row(norm_gain[1, 0 if sub == 1 else 2])).then_inc(gain_in, 16)
                for q in x_stored:
                    pool.wait_ge(q, 16 * TH * sub)
                for t in range(TH):
                    pool.dma_start(x_st0[:, t, :], x_scr[t]).then_inc(x_in[t], 16)
                for t in range(TH):
                    n = TT * sub + t
                    dst = x_scr[t] if sub < LAST else out[0, t * P:(t + 1) * P, :]
                    add_and_store(t, n, x_st0[:, t, :], y_st0[:, t, :], dst)
                pool.wait_ge(gs_split, half1_step)
                for t in range(TH, TT):
                    pool.dma_start(x_st1[:, t - TH, :], x_scr[t]).then_inc(x_in[t], 16)
                if sub == 1:
                    pool.wait_ge(gs_split, 2 * FT)
                    pool.wait_ge(ang_stored, 16 * 8)
                    pool.dma_start(sin_t[:, :], ang_scr[0]).then_inc(ang_in, 16)
                    pool.dma_start(cos_t[:, :], ang_scr[1]).then_inc(ang_in, 16)
                for t in range(TH, TT):
                    n = TT * sub + t
                    dst = x_scr[t] if sub < LAST else out[0, t * P:(t + 1) * P, :]
                    add_and_store(t, n, x_st1[:, t - TH, :], y_st1[:, t - TH, :], dst)

            chain = Tally(pool, pool_chain)
            ts, tt = pool.tensor_scalar, pool.tensor_tensor
            pool.wait_ge(h_done, TT)
            pool.wait_ge(small_in, 16)
            for q in range(seq // AW):
                cols = slice(AW * q, AW * (q + 1))
                pool.dma_start(pos_i[:, :], positions[:, cols].broadcast_to([P, AW])).then_inc(pos_in, 16)
                pool.wait_ge(pos_in, 16 * q + 16)
                chain.mark(pool.tensor_copy(ang_a[:, :], pos_i[:, :]))
                chain.wait()
                chain.mark(ts(ang_a[:, :], ang_a[:, :], inv_freq, None, ALU.mult))
                chain.wait()
                for unit in (TURNS, 1.0):
                    chain.mark(ts(ang_b[:, :], ang_a[:, :], 1.0 / (2.0 * np.pi * unit), ROUND, ALU.mult, ALU.add))
                    chain.wait()
                    chain.mark(ts(ang_b[:, :], ang_b[:, :], ROUND, None, ALU.subtract))
                    chain.wait()
                    for part in two_pi_parts():
                        chain.mark(ts(ang_c[:, :], ang_b[:, :], part * unit, None, ALU.mult))
                        chain.wait()
                        chain.mark(tt(ang_a[:, :], ang_a[:, :], ang_c[:, :], ALU.subtract))
                        chain.wait()
                chain.mark(ts(ang_b[:, :], ang_a[:, :], float(np.pi / 2), None, ALU.add))
                chain.wait()
                chain.mark(ts(ang_c[:, :], ang_b[:, :], float(np.pi), 2.0 * float(np.pi), ALU.is_gt, ALU.mult))
                chain.wait()
                chain.mark(tt(ang_b[:, :], ang_b[:, :], ang_c[:, :], ALU.subtract))
                chain.wait()
                pi32 = 3.1415925
                ts(ang_a[:, :], ang_a[:, :], pi32, -pi32, ALU.min, ALU.max).then_inc(ang_done, 1)
                ts(ang_b[:, :], ang_b[:, :], pi32, -pi32, ALU.min, ALU.max).then_inc(ang_done, 1)
                pool.wait_ge(ang_done, 2 * q + 2)
                pool.dma_start(ang_scr[0][:, cols], ang_a[:, :]).then_inc(ang_stored, 16)
                pool.dma_start(ang_scr[1][:, cols], ang_b[:, :]).then_inc(ang_stored, 16)
                pool.wait_ge(ang_stored, 32 * q + 32)
            residuals(1, down0, FT + 12)

            def store_head(h):
                for j in range(HV):
                    pool.wait_ge(yt_done, HV * h + j + 1)
                    pool.dma_start(y_scr[bass.ds(HV * h + j, 1)].rearrange("o p n -> p (o n)") if h is not HEADS - 1
                                   else y_scr[HV * h + j], gate[:, j, :]).then_inc(yt_stored, 16)

            def bring_back(h):
                for j in range(HV):
                    f = HV * h + j
                    pool.dma_start(g_t[:, y_pos(f), :], y_scr[f]).then_inc(y_back[h], 16)

            pool.memset(flag_t[:, :], 0.0).then_inc(gate_free, 1)
            with turns(pool, HEADS - 1) as h:
                store_head(h)
                pool.wait_ge(yt_stored, 16 * HV * h + 16 * HV)
                pool.tensor_tensor(flag_t[:, :], flag_t[:, :], flag_t[:, :], ALU.add).then_inc(gate_free, 1)
            pool.wait_ge(slice_done, out0 - 3)
            pool.wait_ge(yt_stored, 16 * (HEADS - 1) * HV)
            for h in range(HEADS - 1):
                bring_back(h)
            store_head(HEADS - 1)
            pool.wait_ge(yt_stored, 16 * VT)
            bring_back(HEADS - 1)
            residuals(2, out0, 2 * FT + VT + 12)
            residuals(3, down1, 2 * FT + 2 * VT + FT + 12)
            pool.wait_ge(out_done, 16 * TT)
            for q in x_stored:
                pool.wait_ge(q, 16 * TH * LAST)

        @block.tensor
        def _(pe):
            mm = pe.matmul

            def three(dst, lhs, rhs, start, stop):
                mm(dst, lhs[0], rhs[0], start=start, stop=False)
                mm(dst, lhs[0], rhs[1], start=False, stop=False)
                return mm(dst, lhs[1], rhs[0], start=False, stop=stop)

            def w_cols(w, r, k):
                return w[:, r, k * P:(k + 1) * P]

            def project_half(r, bank, half):
                for k in range(KT):
                    last = three(ps[:, bank + half, :], (w_cols(w_hi, r, k), w_cols(w_lo, r, k)),
                                 (a_hi[:, half, k, :], a_lo[:, half, k, :]), k == 0, k == KT - 1)
                return last

            def project(s, r, bank):
                pe.wait_ge(w_split, s + 1)
                project_half(r, bank, 0)
                project_half(r, bank, 1).then_inc(slice_done, 1)

            def transposes(n, src, bank):
                pe.wait_ge(h_done, n + 1)
                for k in range(KT):
                    last = pe.transpose(pair(bank)[:, k * P:(k + 1) * P], src[:, k * P:(k + 1) * P], ident)
                last.then_inc(tr_done, 1)

            def pool_mix(t):
                pe.wait_ge(mix_scaled, t + 1)
                if t:
                    pe.wait_ge(d_split, t)
                for c in range(KT):
                    g = c // GC
                    dst = pair(0)[:, c * P:(c + 1) * P]
                    last = mm(dst, x_p[:, t, c * P:(c + 1) * P], mix[:, t % 4, g * P:(g + 1) * P],
                              start=True, stop=(t == 0))
                    if t:
                        p0 = G * P + g * WMAX
                        last = mm(dst[:, 0:WMAX], x_p[:, t - 1, c * P:(c + 1) * P], mix[:, (t - 1) % 4, p0:p0 + WMAX],
                                  start=False, stop=True)
                last.then_inc(pool_done, 1)

            def pool_project(t):
                pe.wait_ge(d_split, t + 1)
                if t == 0:
                    pe.wait_ge(pw_split, 1)
                if t == 1:
                    pe.wait_ge(taps_out, 1)
                if t >= 2:
                    pe.wait_ge(x1_done, t - 1)
                dst = pair(2 + 4 * (t % 2))
                for g in range(G):
                    for c in range(GC):
                        k = g * GC + c
                        last = three(dst[:, g * GW:(g + 1) * GW], (a_cols(a_hi, t)[:, k, :], a_cols(a_lo, t)[:, k, :]),
                                     (pw_hi[:, k, :], pw_lo[:, k, :]), c == 0, c == GC - 1)
                last.then_inc(y_done, 1)

            pe.wait_ge(small_in, 16)
            pe.wait_ge(rows_in, 16)
            pe.transpose(ps[:, 6, 0:KT], gain_rows[0:KT, :], ident[0:KT, 0:KT]).then_inc(par_done, 1)

            for step in range(TT + 4):
                if 0 <= step - 1 < TT:
                    pool_mix(step - 1)
                if step == 1:
                    pe.wait_ge(const_in, 16 * 5)
                    for j in range(8):
                        pe.transpose(ps[:, 7, j * UP:(j + 1) * UP], par_rows[0:UP, j, :], ident[0:UP, 0:UP])
                    pe.transpose(ps[:, 7, 8 * UP:8 * UP + VT], gn_rows[0:VT, :], ident[0:VT, 0:VT]).then_inc(par_done, 1)
                if 0 <= step - 2 < TT:
                    pool_project(step - 2)
                t = step - 4
                if 0 <= t < TT:
                    if t >= 1:
                        pe.wait_ge(a_done, t)
                    transposes(t, y_stp[:, t % 4, :], 4)

            def up(sub, up_base):
                layer = sub // 2
                first_tile = UP * layer
                n0 = TT * sub
                for r in range(2):
                    pe.wait_ge(w_split, up_base + r + 1)
                    if r == 0:
                        pe.wait_ge(a_done, n0 - TH)
                    project_half(r, 2 * r, 0)
                if sub == LAST:
                    late_transposes(sub - 1)
                pe.wait_ge(a_done, n0)
                for r in range(2):
                    project_half(r, 2 * r, 1).then_inc(slice_done, 1)
                with turns(pe, FT - 1) as i:
                    for r in range(2):
                        pe.wait_ge(conv_done, first_tile + 2 * i + r + 1)
                        project(up_base + 2 * i + 2 + r, r, 2 * r)

            def down(down_base, nk, g_base, sub):
                hi, lo = (gs_hi_r, gs_lo_r) if sub == 2 else (gs_hi, gs_lo)

                def tile(half, t, r, first, last):
                    for n in range(2):
                        cols = slice(n * HALF, (n + 1) * HALF)
                        ins = three(ps[:, bank_of(sub, half, t) + n, :],
                                    (hi[:, r, t * P:(t + 1) * P], lo[:, r, t * P:(t + 1) * P]),
                                    (w_hi[:, r, cols], w_lo[:, r, cols]), first, last)
                    return ins

                def operands(s, g):
                    pe.wait_ge(w_split, s + 1)
                    pe.wait_ge(gs_split, g + 1)

                def bank_free(half, t):
                    if half == 1:
                        count = TH * (sub - 1) + (TH - 1, TH, TH, TH)[t]
                        pe.wait_ge(drained_a, count)
                        pe.wait_ge(drained_v, count)
                    elif sub == 2:
                        if t == 1:
                            pe.wait_ge(gate_done, HV * HEADS)
                        else:
                            pe.wait_ge(yt_done, HV * (HEADS - 1) + max(t + 1, 2))
                    elif t >= 2:
                        pe.wait_ge(conv_done, UP * (1 + sub // 2) + t - 3)

                def norm_transposes(t):
                    if t < 2:
                        pe.wait_ge(yn_done, TT * sub + TH + t + 1)
                    else:
                        pe.wait_ge(a_done, TT * sub + t - 1)
                    transposes(TT * sub + t, y_st0[:, t, :], 2 * (t % 2))

                for half in range(2):
                    s0, g0 = down_base + half * nk, g_base + half * nk
                    for k in range(2):
                        operands(s0 + k, g0 + k)
                        for t in range(TH):
                            if k == 0:
                                bank_free(half, t)
                            ins = tile(half, t, k, k == 0, False)
                        ins.then_inc(slice_done, 1)
                    with turns(pe, (nk - 4) // 2) as i:
                        for u in range(2):
                            operands(s0 + 2 + 2 * i + u, g0 + 2 + 2 * i + u)
                            for t in range(TH):
                                ins = tile(half, t, u, False, False)
                            ins.then_inc(slice_done, 1)
                    if half == 0:
                        operands(s0 + nk - 2, g0 + nk - 2)
                        for t in range(TH):
                            ins = tile(half, t, 0, False, False)
                        ins.then_inc(slice_done, 1)
                        operands(s0 + nk - 1, g0 + nk - 1)
                        for t in range(TH):
                            tile(half, t, 1, False, True).then_inc(y_done if t < TH - 1 else slice_done, 1)
                        continue
                    operands(s0 + nk - 1, g0 + nk - 1)
                    for t in range(TH):
                        ins = tile(half, t, 0, False, False)
                        if t == TH - 1:
                            ins.then_inc(slice_done, 1)
                        tile(half, t, 1, False, True).then_inc(y_done if t < TH - 1 else slice_done, 1)
                        if sub < LAST:
                            for u in {1: (0,), 2: (1,), 3: (2, 3)}.get(t, ()):
                                norm_transposes(u)

            def late_transposes(sub):
                for t in range(TH, TT):
                    pe.wait_ge(a_done, TT * sub + t - 1)
                    transposes(TT * sub + t, y_st1[:, t - TH, :], late_bank(t))

            up(1, up0)
            down(down0, FT, 0, 1)

            def scores(h, m, half, j):
                lead = max(0, j - TH * half) * P
                if m >= 2:
                    pe.wait_ge(s_split, n_items * h + m - 1)
                dst = ps[:, 4 + m % 2, lead:HALF]
                for c in range(2):
                    jk, jc = j // TH, slice((j % TH) * P, (j % TH + 1) * P)
                    last = three(dst, (k_s[:, jk, 0, c, jc], k_s[:, jk, 1, c, jc]),
                                 (q_s[:, half, 0, c, lead:HALF], q_s[:, half, 1, c, lead:HALF]), c == 0, c == 1)
                last.then_inc(s_done, 1)

            def values(h, m, half, j):
                pe.wait_ge(s_split, n_items * h + m + 1)
                for i in range(max(j, TH * half), TH * half + TH):
                    if half == 1 and j == 0 and i >= TH + 2:
                        pe.wait_ge(o_copied, TT * h + i - TH - 1)
                    cols = slice((i - TH * half) * P, (i - TH * half + 1) * P)
                    dst = ps[:, (i if half == 0 else (i + 2) % 8), :]
                    last = three(dst, (s_hi[:, m % 2, cols], s_lo[:, m % 2, cols]),
                                 (v_hi[:, j, :], v_lo[:, j, :]), j == 0, j == i)
                    if i == j:
                        last.then_inc(o_done, 1)

            items = [(half, j) for half in range(2) for j in range(TH * half + TH)]
            n_items = len(items)

            def head(h):
                s = ret0 + HEAD_SLICES * h
                if isinstance(h, int):
                    pe.wait_ge(a_done, TT + TH)
                    for u in range(2):
                        pe.wait_ge(w_split, s + u + 1)
                        project_half(u, 2 * u, 0)
                    late_transposes(1)
                    pe.wait_ge(a_done, 2 * TT)
                    for u in range(2):
                        project_half(u, 2 * u, 1).then_inc(slice_done, 1)
                else:
                    pe.wait_ge(yt_done, HV * h - HV + 2)
                    project(s, 0, 0)
                    pe.wait_ge(yt_done, HV * h)
                    project(s + 1, 1, 2)
                for u in range(2, 4):
                    project(s + u, u % 2, 2 * u)
                for u in range(4):
                    pe.wait_ge(w_split, s + 4 + u + 1)
                    for t in range(TT):
                        if u == 0 and t in (0, 4, 6):
                            pe.wait_ge(rot_copied, 4 * h + {0: 2, 4: 3, 6: 4}[t])
                        for c in range(2):
                            k, r = 2 * u + c, u % 2
                            last = three(ps[:, t, :], (a_cols(a_hi, t)[:, k, :], a_cols(a_lo, t)[:, k, :]),
                                         (w_hi[:, r, c * HALF:(c + 1) * HALF], w_lo[:, r, c * HALF:(c + 1) * HALF]),
                                         k == 0, k == KT - 1)
                        if u == 3 and t < TT - 1:
                            last.then_inc(v_done, 1)
                    last.then_inc(slice_done, 1)
                pe.wait_ge(rot_split, 2 * h + 2)
                pe.wait_ge(v_split, TT * h + 6)
                scores(h, 0, *items[0])
                for m, (half, j) in enumerate(items):
                    if m + 1 < n_items:
                        scores(h, m + 1, *items[m + 1])
                    if (half, j) == (1, 0):
                        pe.wait_ge(v_split, TT * h + TT)
                    values(h, m, half, j)
                def turn(j, bank):
                    dst = pair(bank)
                    for t in range(TT):
                        last = pe.transpose(dst[:, t * P:(t + 1) * P], o_s[:, t, j * P:(j + 1) * P], ident)
                    last.then_inc(ot_done, 1)

                pe.wait_ge(o_copied, TT * h + TH)
                project(s + 8, 0, 2)
                project(s + 9, 1, 4)
                pe.wait_ge(gn_done, TT * h + TT)
                turn(0, 6)
                turn(1, 0)
                pe.wait_ge(gate_done, HV * h + 1)
                project(s + 10, 0, 2)
                pe.wait_ge(yt_done, HV * h + 1)
                turn(2, 6)
                pe.wait_ge(gate_done, HV * h + 2)
                project(s + 11, 1, 4)
                pe.wait_ge(gate_done, HV * h + 3)
                turn(3, 2)

            head(0)
            with turns(pe, HEADS - 1) as i:
                head(i + 1)
            down(out0, VT, 2 * FT, 2)
            up(3, up1)
            down(down1, FT, 2 * FT + 2 * VT, 3)

        @block.scalar
        def _(act):
            run = act.activation
            chain = Tally(act, act_chain)

            def split_w(s, slot):
                act.wait_ge(raw_full[slot], 16 * (s // 4 + 1))
                run(w_hi[:, slot % 2, :], w_raw[:, slot, :], ACT.Copy).then_inc(w_hi_done, 1)

            def split_loop(turn, first, u, after):
                act.wait_ge(slice_done, after)
                act.wait_ge(raw_full[(first + u) % 4], 16 * ((first + u) // 4 + 1) + 16 * turn)
                run(w_hi[:, (first + u) % 2, :], w_raw[:, (first + u) % 4, :], ACT.Copy).then_inc(w_hi_done, 1)

            def split_g(dst, src, r):
                run(dst[:, r, :], src, ACT.Copy).then_inc(gs_hi_done, 1)

            def root(n, src, col, done):
                t = n % TT
                chain.mark(run(junk[:, :], src, ACT.Square, accum_out=stat[:, t, col:col + 1]))
                chain.wait()
                run(stat[:, t, col + 1:col + 2], stat[:, t, col:col + 1], ACT.Sqrt,
                    scale=1.0 / d, bias=stat[:, 0, 7:8]).then_inc(done, 1)

            def norm_x(n, x_sb):
                act.wait_ge(x1_done, n + 1)
                root(n, x_sb, 3, x_root)

            def take_transposes(n, bank):
                act.wait_ge(tr_done, n + 1)
                run(a_cols(a_hi, n % TT), pair(bank).rearrange("p (k n) -> p k n", k=KT), ACT.Copy).then_inc(a_hi_done, 1)

            act.dma_start(mix_m[:, :], pool_tables).then_inc(mix_in, 16)
            act.dma_start(small[:, :], small_tables).then_inc(small_in, 16)
            act.dma_start(pw_raw[:, :, :], pool_w[0].rearrange("g (c p) n -> p (g c) n", p=P)).then_inc(pw_in, 16)
            act.wait_ge(eps_done, 1)
            for t in range(TT + 4):
                if t < TT:
                    act.wait_ge(x_first[t], 16)
                    chain.mark(run(junk[:, :], x_p[:, t, :], ACT.Square, accum_out=stat[:, t, 0:1]))
                    chain.wait()
                    run(stat[:, t, 1:2], stat[:, t, 0:1], ACT.Sqrt, scale=1.0 / d, bias=stat[:, 0, 7:8]).then_inc(x0_root, 1)
                if t == 1:
                    act.wait_ge(pw_scaled, 1)
                    run(pw_hi[:, :, :], pw_raw[:, :, :], ACT.Copy).then_inc(pw_hi_done, 1)
                u = t - 1
                if 0 <= u < TT:
                    act.wait_ge(pool_done, u + 1)
                    run(a_cols(a_hi, u), pair(0).rearrange("p (k n) -> p k n", k=KT), ACT.Copy).then_inc(d_hi_done, 1)
                if t == TT - 1:
                    split_w(0, 0)
                    split_w(1, 1)
                u = t - 2
                if 0 <= u < TT:
                    act.wait_ge(y_done, u + 1)
                    root(u, pair(2 + 4 * (u % 2)), 0, y_root)
                u = t - 3
                if 0 <= u < TT:
                    norm_x(u, x_p[:, u, :])
                u = t - 4
                if 0 <= u < TT:
                    take_transposes(u, 4)

            def up(sub, up_base):
                layer = sub // 2
                tile0, pair0 = UP * layer, FT * layer
                par = taps[:, layer, :, :]

                def body(turn, i, u2, slot_first, first=False, last=False):
                    s = up_base + 2 * i

                    def tap(z):
                        col = z * FT + i
                        run(conv[:, z, :], pair(2 * z), ACT.Identity,
                            scale=par[:, 2, bass.ds(col, 1)], bias=par[:, 3, bass.ds(col, 1)]).then_inc(tap_done, 1)

                    split_loop(turn, slot_first, 2 * u2, s + 1)
                    if not first:
                        act.wait_ge(mult_done, pair0 + i)
                    tap(0)
                    act.wait_ge(conv_done, tile0 + 2 * i + 1)
                    run(conv[:, 0, :], conv[:, 0, :], ACT.Silu).then_inc(silu_done, 1)
                    if last:
                        for k in range(2):
                            split_g(gs_hi, hidden(k, 0), k)
                        act.wait_ge(slice_done, s + 2)
                        tap(1)
                        split_loop(turn, slot_first, 2 * u2 + 1, s + 2)
                    else:
                        split_loop(turn, slot_first, 2 * u2 + 1, s + 2)
                        tap(1)

                act.wait_ge(taps_out, 1)
                for i in range(2):
                    body(0, i, i, up_base + 2, first=(i == 0))
                with turns(act, FT // 2 - 2) as i:
                    for u2 in range(2):
                        body(i, 2 * i + 2 + u2, u2, up_base + 6)
                for u2 in range(2):
                    body(0, FT - 2 + u2, u2, up_base + UP - 2, last=(u2 == 1))

            def down(down_base, nk, g_base, sub, g_src):
                layer = sub // 2
                dst = gs_hi_r if sub == 2 else gs_hi
                if sub != 2:
                    act.wait_ge(mult_done, FT * (1 + layer))

                def g_split(k, half, r):
                    if sub == 2 and half == 0 and k % HV == 0:
                        act.wait_ge(y_back[k // HV], 16 * HV)
                    split_g(dst, g_src(k, half), r)

                def split_ahead(s, turn=0, slot_first=None, u=0):
                    split_loop(turn, s + 2 if slot_first is None else slot_first, u, s + 1)

                if sub == 2:
                    for k in range(2):
                        g_split(k, 0, k)
                for half in range(2):
                    s0, end = down_base + half * nk, down_base + half * nk + nk
                    if half == 1 and sub == 2:
                        act.wait_ge(yt_stored, 16 * VT)
                    straight, n_loop = plan_steps(nk, half, sub)
                    for k in range(straight):
                        split_ahead(s0 + k)
                        g_split(k + 2, half, k % 2)
                        if half == 1:
                            first_half_norms(sub, k)
                    if n_loop:
                        with turns(act, n_loop) as i:
                            for u in range(4):
                                k = straight + 4 * i + u
                                split_ahead(s0 + k, i, s0 + straight + 2, u)
                                split_g(dst, g_src(k + 2, half), (straight + u) % 2)
                    if half == 0:
                        split_ahead(end - 2)
                        g_split(0, 1, 0)
                        for t in range(TH):
                            tile_ended(sub, half, t, end)
                            run(y_st0[:, t, 0:HALF], ps[:, bank_of(sub, 0, t), :], ACT.Copy).then_inc(drained_a, 1)
                        split_ahead(end - 1)
                        g_split(1, 1, 1)

                def y_norm(t):
                    tile_ended(sub, 1, t, end)
                    root(TT * sub + TH + t, pair(bank_of(sub, 1, t)), 0, y_root)

                def x_norm(t):
                    norm_x(TT * sub + TH + t, x_st1[:, t, :])

                if sub == LAST:
                    for t in range(TH):
                        y_norm(t)
                    return
                y_norm(0)
                y_norm(1)
                take_transposes(TT * sub, 0)
                take_transposes(TT * sub + 1, 2)
                split_ahead(end - 2)
                y_norm(2)
                take_transposes(TT * sub + 2, 0)
                take_transposes(TT * sub + 3, 2)
                y_norm(3)
                split_ahead(end - 1)
                x_norm(0)
                x_norm(1)
                for t in range(TH):
                    if t + 2 < TH:
                        if t:
                            take_transposes(TT * sub + TH + t - 1, late_bank(t - 1))
                        x_norm(t + 2)
                for t in range(1, TH):
                    take_transposes(TT * sub + TH + t, late_bank(t))

            def tile_ended(sub, half, t, end):
                if t < TH - 1:
                    act.wait_ge(y_done, TT + (TH - 1) * (2 * (sub - 1) + half) + t + 1)
                else:
                    act.wait_ge(slice_done, end)

            def first_half_norms(sub, k):
                t = k // 2
                if t < TH:
                    n = TT * sub + t
                    if k % 2 == 0:
                        act.wait_ge(drained_v, TH * (sub - 1) + t + 1)
                        act.wait_ge(drained_a, TH * (sub - 1) + t + 1)
                        root(n, y_st0[:, t, :], 0, y_root)
                    elif sub < LAST:
                        norm_x(n, x_st0[:, t, :])

            up(1, up0)
            down(down0, FT, 0, 1, hidden)

            act.wait_ge(ang_in, 32)
            run(sin_t[:, :], sin_t[:, :], ACT.Sin).then_inc(sin_done, 1)
            run(cos_t[:, :], cos_t[:, :], ACT.Sin).then_inc(sin_done, 1)
            items = [(half, j) for half in range(2) for j in range(TH * half + TH)]
            n_items = len(items)
            per_head = 0
            with turns(act, HEADS) as h:
                s = ret0 + HEAD_SLICES * h

                def ahead(u):
                    act.wait_ge(slice_done, s + u - 1)
                    act.wait_ge(raw_full[u % 4], 16 * ((ret0 + u) // 4 + 1) + 16 * (HEAD_SLICES // 4) * h)
                    run(w_hi[:, u % 2, :], w_raw[:, u % 4, :], ACT.Copy).then_inc(w_hi_done, 1)

                def high_parts(which, dst):
                    act.wait_ge(rot_f32, 2 * h + which + 1)
                    for c in range(2):
                        ins = run(dst[:, :, 0, c, :], rot[:, 2 + c, :].rearrange("p (b n) -> p b n", b=2), ACT.Copy)
                    ins.then_inc(rot_hi, 1)

                for u in range(4):
                    ahead(u + 2)
                    if u == 0:
                        act.wait_ge(gate_free, h + 1)
                    if u == 2:
                        high_parts(0, q_s)
                    run(rot[:, u % 2, :], pair(2 * u), ACT.Copy).then_inc(rot_copied, 1)
                ahead(6)
                high_parts(1, k_s)
                ahead(7)
                ahead(8)
                for t in range(TT):
                    if t < TT - 1:
                        act.wait_ge(v_done, (TT - 1) * h + t + 1)
                    else:
                        act.wait_ge(slice_done, s + 8)
                    run(v_hi[:, t, :], ps[:, t, :], ACT.Copy,
                        scale=v_decay[:, bass.ds(TT * h + t, 1)]).then_inc(v_hi_done, 1)
                ahead(9)

                def copy_out(i):
                    act.wait_ge(o_done, TT * h + i + 1)
                    run(o_s[:, i, :], ps[:, (i if i < TH else (i + 2) % 8), :], ACT.Copy,
                        scale=out_decay[:, bass.ds(TT * h + i, 1)]).then_inc(o_copied, 1)

                for m, (half, j) in enumerate(items):
                    lead = max(0, j - TH * half) * P
                    act.wait_ge(s_done, n_items * h + m + 1)
                    run(s_hi[:, m % 2, lead:HALF], ps[:, 4 + m % 2, lead:HALF], ACT.Copy).then_inc(s_hi_done, 1)
                    if m == TH:
                        copy_out(0)
                        copy_out(1)
                    if m == TH + 1:
                        copy_out(2)
                        copy_out(3)
                for i in range(TH, TT):
                    copy_out(i)
                for j in range(HV):
                    ahead(10 + j)
                    act.wait_ge(rot_split, 2 * h + 2)
                    run(gate[:, j, :], pair(2 + 2 * (j % 2)), ACT.Silu).then_inc(gate_done, 1)
                    if j == 0:
                        act.wait_ge(gn_var, h + 1)
                        run(gn_root[:, :], mv[:, :, 1], ACT.Sqrt, scale=1.0, bias=stat[:, 0, 7:8]).then_inc(gn_root_done, 1)
            down(out0, VT, 2 * FT, 2, heads_out)
            up(3, up1)
            down(down1, FT, 2 * FT + 2 * VT, 3, hidden)

        @block.vector
        def _(dve):
            chain = Tally(dve, dve_chain)
            tt, stt = dve.tensor_tensor, dve.scalar_tensor_tensor

            def split_w(s, slot):
                dve.wait_ge(w_hi_done, s + 1)
                tt(w_lo[:, slot % 2, :], w_raw[:, slot, :], f32(w_hi[:, slot % 2, :]), ALU.subtract).then_inc(w_split, 1)

            def split_g(parts, g, src, r):
                dve.wait_ge(gs_hi_done, g + 1)
                tt(parts[1][:, r, :], src, f32(parts[0][:, r, :]), ALU.subtract).then_inc(gs_split, 1)

            def rstd(t, col):
                chain.mark(dve.reciprocal(stat[:, t, col + 2:col + 3], stat[:, t, col + 1:col + 2]))
                chain.wait()
                return stat[:, t, col + 2:col + 3]

            def norm_y(n, src, y_sb, x_sb):
                t = n % TT
                dve.wait_ge(y_root, n + 1)
                stt(out=y_sb, in0=src, scalar=rstd(t, 0), in1=gain_post[:, :],
                    op0=ALU.mult, op1=ALU.mult).then_inc(yn_done, 1)
                if not pool_adds(n):
                    dve.wait_ge(x_in[t], 16 * (n // TT))
                    dve.wait_ge(yn_done, n + 1)
                    tt(x_sb, x_sb, y_sb, ALU.add).then_inc(x1_done, 1)

            def norm_h(n, x_sb, y_sb):
                dve.wait_ge(x_root, n + 1)
                stt(out=y_sb, in0=x_sb, scalar=rstd(n % TT, 3), in1=gain_pre[:, :],
                    op0=ALU.mult, op1=ALU.mult).then_inc(h_done, 1)

            def take_transposes(n, bank):
                if n % TT >= TH and n >= TT:
                    dve.wait_ge(x_stored[0], 16 * TH * (n // TT + 1))
                dve.wait_ge(a_hi_done, n + 1)
                tt(a_cols(a_lo, n % TT), pair(bank).rearrange("p (k n) -> p k n", k=KT),
                   f32(a_cols(a_hi, n % TT)), ALU.subtract).then_inc(a_done, 1)

            dve.memset(stat[:, 0, 7:8], EPS).then_inc(eps_done, 1)
            dve.wait_ge(mix_in, 16)
            for t in range(TT + 4):
                if t < TT:
                    dve.wait_ge(x0_root, t + 1)
                    if t >= 4:
                        dve.wait_ge(pool_done, t - 2)
                    scale = rstd(t, 0)
                    if t == 0:
                        dve.tensor_scalar(mix[:, 0, 0:G * P], mix_m[:, MIX:MIX + G * P], scale, None, ALU.mult)
                        ins = dve.tensor_scalar(mix[:, 0, G * P:MIX], mix_m[:, G * P:MIX], scale, None, ALU.mult)
                    else:
                        ins = dve.tensor_scalar(mix[:, t % 4, :], mix_m[:, 0:MIX], scale, None, ALU.mult)
                    ins.then_inc(mix_scaled, 1)
                if t == 1:
                    dve.wait_ge(par_done, 1)
                    chain.mark(dve.tensor_copy(gain_first[:, :], ps[:, 6, 0:KT]))
                    dve.wait_ge(pw_in, 16)
                    dve.wait_ge(scale_in, 16)
                    chain.wait()
                    for k in range(KT):
                        g = k // GC
                        ins = stt(out=pw_raw[:, k, :], in0=pw_raw[:, k, :], scalar=gain_first[:, k:k + 1],
                                  in1=pool_scale_b[:, g * GW:(g + 1) * GW], op0=ALU.mult, op1=ALU.mult)
                    ins.then_inc(pw_scaled, 1)
                    dve.wait_ge(pw_hi_done, 1)
                    tt(pw_lo[:, :, :], pw_raw[:, :, :], f32(pw_hi[:, :, :]), ALU.subtract).then_inc(pw_split, 1)
                if t == 1:
                    dve.wait_ge(par_done, 2)
                    dve.tensor_copy(taps[:, :, :, :].rearrange("p l a t -> p (l a t)"), ps[:, 7, 0:8 * UP])
                    dve.tensor_copy(gn_gain[:, :], ps[:, 7, 8 * UP:8 * UP + VT]).then_inc(taps_out, 1)
                if t == TT - 1:
                    split_w(0, 0)
                    split_w(1, 1)
                u = t - 1
                if 0 <= u < TT:
                    dve.wait_ge(d_hi_done, u + 1)
                    tt(a_cols(a_lo, u), pair(0).rearrange("p (k n) -> p k n", k=KT), f32(a_cols(a_hi, u)),
                       ALU.subtract).then_inc(d_split, 1)
                u = t - 2
                if 0 <= u < TT:
                    if u == 0:
                        dve.wait_ge(gain_in, 32)
                    if u >= 4:
                        dve.wait_ge(tr_done, u - 3)
                    norm_y(u, pair(2 + 4 * (u % 2)), y_stp[:, u % 4, :], x_p[:, u, :])
                u = t - 3
                if 0 <= u < TT:
                    norm_h(u, x_p[:, u, :], y_stp[:, u % 4, :])
                u = t - 4
                if 0 <= u < TT:
                    take_transposes(u, 4)

            def up(sub, up_base, g_base):
                layer = sub // 2
                tile0, pair0 = UP * layer, FT * layer
                par = taps[:, layer, :, :]
                for q in x_stored:
                    dve.wait_ge(q, 16 * TH * sub)

                def body(i, slot, last=False):
                    def older_taps(z):
                        tile = tile0 + 2 * i + z
                        dve.wait_ge(tap_done, tile + 1)
                        col = z * FT + i
                        for back in (1, 2):
                            ins = stt(out=conv[:, z, back:], in0=pair(2 * z)[:, 0:seq - back],
                                      scalar=par[:, 2 - back, bass.ds(col, 1)], in1=conv[:, z, back:],
                                      op0=ALU.mult, op1=ALU.add)
                            if back == 1:
                                chain.mark(ins)
                                chain.wait()
                        ins.then_inc(conv_done, 1)

                    split_w(up_base + 2 * i + 2, slot)
                    older_taps(0)
                    if last:
                        for k in range(2):
                            split_g((gs_hi, gs_lo), g_base + k, hidden(k, 0), k)
                        older_taps(1)
                        split_w(up_base + 2 * i + 3, slot + 1)
                    else:
                        split_w(up_base + 2 * i + 3, slot + 1)
                        older_taps(1)
                    dve.wait_ge(silu_done, pair0 + i + 1)
                    dve.wait_ge(conv_done, tile0 + 2 * i + 2)
                    tt(g_t[:, bass.ds(i, 1), :].rearrange("p o n -> p (o n)"), conv[:, 0, :], conv[:, 1, :],
                       ALU.mult).then_inc(mult_done, 1)

                with turns(dve, FT // 2 - 1, chain, 4) as turn:
                    for u2 in range(2):
                        body(2 * turn + u2, (up_base + 2 * u2 + 2) % 4)
                for u2 in range(2):
                    body(FT - 2 + u2, (up_base + 2 * u2 + 2) % 4, last=(u2 == 1))

            def tile_ended(sub, half, t, end):
                if t < TH - 1:
                    dve.wait_ge(y_done, TT + (TH - 1) * (2 * (sub - 1) + half) + t + 1)
                else:
                    dve.wait_ge(slice_done, end)

            def down(down_base, nk, g_base, sub, g_src):
                parts = (gs_hi_r, gs_lo_r) if sub == 2 else (gs_hi, gs_lo)
                if sub == 2:
                    for k in range(2):
                        split_g(parts, g_base + k, g_src(k, 0), k)
                for half in range(2):
                    s0, g0 = down_base + half * nk, g_base + half * nk
                    end = s0 + nk
                    straight, n_loop = plan_steps(nk, half, sub)
                    for k in range(straight):
                        split_w(s0 + k + 2, (s0 + k + 2) % 4)
                        split_g(parts, g0 + k + 2, g_src(k + 2, half), k % 2)
                        if half == 1:
                            first_half_norms(sub, k)
                    if n_loop:
                        with turns(dve, n_loop) as i:
                            for u in range(4):
                                k = straight + 4 * i + u
                                split_w(s0 + k + 2, (s0 + straight + 2 + u) % 4)
                                split_g(parts, g0 + k + 2, g_src(k + 2, half), (straight + u) % 2)
                    if half == 0:
                        split_w(end, end % 4)
                        split_g(parts, g0 + nk, g_src(0, 1), 0)
                        for t in range(TH):
                            tile_ended(sub, half, t, end)
                            dve.tensor_copy(y_st0[:, t, HALF:d], ps[:, bank_of(sub, 0, t) + 1, :]).then_inc(drained_v, 1)
                        split_w(end + 1, (end + 1) % 4)
                        split_g(parts, g0 + nk + 1, g_src(1, 1), 1)

                def y_norm(t):
                    norm_y(TT * sub + TH + t, pair(bank_of(sub, 1, t)), y_st1[:, t, :], x_st1[:, t, :])

                def x_norm(t):
                    norm_h(TT * sub + TH + t, x_st1[:, t, :], y_st1[:, t, :])

                def take(t):
                    take_transposes(TT * sub + t, 2 * (t % 2) if t < TH else late_bank(t))

                if sub == LAST:
                    for t in range(TH):
                        y_norm(t)
                    return
                y_norm(0)
                y_norm(1)
                take(0)
                take(1)
                split_w(end, end % 4)
                take(2)
                take(3)
                y_norm(2)
                split_w(end + 1, (end + 1) % 4)
                y_norm(3)
                x_norm(0)
                x_norm(1)
                take(4)
                x_norm(2)
                take(5)
                x_norm(3)
                take(6)
                take(7)

            def first_half_norms(sub, k):
                t = k // 2
                if t < TH:
                    n = TT * sub + t
                    if k == 0:
                        dve.wait_ge(gain_in, 32 * (sub + 1) if sub < LAST else 32 * sub + 16)
                    if k % 2 == 0:
                        norm_y(n, y_st0[:, t, :], y_st0[:, t, :], x_st0[:, t, :])
                    elif sub < LAST:
                        norm_h(n, x_st0[:, t, :], y_st0[:, t, :])

            up(1, up0, 0)
            down(down0, FT, 0, 1, hidden)

            items = [(half, j) for half in range(2) for j in range(TH * half + TH)]
            n_items = len(items)
            for q in x_stored:
                dve.wait_ge(q, 16 * TH * 2)
            dve.wait_ge(sin_done, 2)
            n_diag = TT
            with turns(dve, HEADS, chain, 2 * 5 + n_diag + TT + 1) as h:
                s = ret0 + HEAD_SLICES * h

                def ahead(u):
                    split_w(s + u, u % 4)

                def rotate(which):
                    dve.wait_ge(rot_copied, 4 * h + 2 * which + 2)
                    if which:
                        dve.wait_ge(rot_split, 2 * h + 1)
                    chain.mark(tt(rot[:, 2, :], rot[:, 0, :], cos_t[:, :], ALU.mult))
                    chain.mark(tt(rot[:, 3, :], rot[:, 1, :], cos_t[:, :], ALU.mult))
                    chain.wait(1)
                    chain.mark(tt(rot[:, 0, :], rot[:, 0, :], sin_t[:, :], ALU.mult))
                    chain.wait(1)
                    chain.mark(tt(rot[:, 1, :], rot[:, 1, :], sin_t[:, :], ALU.mult))
                    chain.wait(1)
                    chain.mark(tt(rot[:, 3, :], rot[:, 3, :], rot[:, 0, :], ALU.add))
                    chain.wait(1)
                    tt(rot[:, 2, :], rot[:, 2, :], rot[:, 1, :], ALU.subtract).then_inc(rot_f32, 1)

                def low_parts(which, dst):
                    dve.wait_ge(rot_hi, 2 * h + which + 1)
                    for c in range(2):
                        ins = tt(dst[:, :, 1, c, :], rot[:, 2 + c, :].rearrange("p (b n) -> p b n", b=2),
                                 f32(dst[:, :, 0, c, :]), ALU.subtract)
                    ins.then_inc(rot_split, 1)

                ahead(2)
                ahead(3)
                rotate(0)
                ahead(4)
                low_parts(0, q_s)
                ahead(5)
                rotate(1)
                ahead(6)
                low_parts(1, k_s)
                ahead(7)
                ahead(8)
                for t in range(TT):
                    dve.wait_ge(v_hi_done, TT * h + t + 1)
                    stt(out=v_lo[:, t, :], in0=ps[:, t, :], scalar=v_decay[:, bass.ds(TT * h + t, 1)],
                        in1=f32(v_hi[:, t, :]), op0=ALU.mult, op1=ALU.subtract).then_inc(v_split, 1)
                ahead(9)
                for m, (half, j) in enumerate(items):
                    lead = max(0, j - TH * half) * P
                    r = m % 2
                    dve.wait_ge(s_hi_done, n_items * h + m + 1)
                    ins = tt(s_lo[:, r, lead:HALF], ps[:, 4 + r, lead:HALF], f32(s_hi[:, r, lead:HALF]), ALU.subtract)
                    if j >= TH * half:
                        chain.mark(ins)
                        chain.wait()
                        diag = slice(lead, lead + P)
                        tt(s_hi[:, r, diag], f32(s_hi[:, r, diag]), causal, ALU.mult)
                        ins = tt(s_lo[:, r, diag], f32(s_lo[:, r, diag]), causal, ALU.mult)
                    ins.then_inc(s_split, 1)
                for i in range(TT):
                    dve.wait_ge(o_copied, TT * h + i + 1)
                    chain.mark(dve.bn_stats(bn6[:, i, :], o_s[:, i, :]))
                chain.wait()
                dve.memset(stat[:, 1, 7:8], 0.0)
                for i in range(TT):
                    ins = dve.bn_aggr(mv[:, i, :], bn6[:, i, :])
                ins.then_inc(gn_var, 1)
                ahead(10)
                dve.wait_ge(gn_root_done, h + 1)
                chain.mark(dve.reciprocal(gn_rstd[:, :], gn_root[:, :]))
                chain.wait()
                for i in range(TT):
                    dve.tensor_scalar(o_s[:, i, :], o_s[:, i, :], mv[:, i, 0:1], gn_rstd[:, i:i + 1],
                                      ALU.subtract, ALU.mult).then_inc(gn_done, 1)
                banks = (6, 0, 6, 2)
                for j in range(HV):
                    if j == 0:
                        ahead(11)
                    if j >= 2:
                        ahead(10 + j)
                    dve.wait_ge(ot_done, HV * h + j + 1)
                    dve.wait_ge(gate_done, HV * h + j + 1)
                    stt(out=gate[:, j, :], in0=pair(banks[j]), scalar=gn_gain[:, bass.ds(HV * h + j, 1)],
                        in1=gate[:, j, :], op0=ALU.mult, op1=ALU.mult).then_inc(yt_done, 1)
            down(out0, VT, 2 * FT, 2, heads_out)
            up(3, up1, 2 * FT + 2 * VT)
            down(down1, FT, 2 * FT + 2 * VT, 3, hidden)


_OUT = ((1, 1024, 1024), "float32")


def kernel(**inputs):
    import concourse.bacc as bacc
    from concourse.bass_utils import run_bass_kernel_spmd

    nc = bacc.Bacc("TRN2", target_bir_lowering=False, num_devices=1)
    pool_tables, small_tables = shape_constants(inputs["x"].shape[1])
    named = dict(inputs)
    named["pool_tables"], named["small_tables"] = pool_tables, small_tables
    arrays, args = {}, {}
    for name, a in named.items():
        a = np.ascontiguousarray(a)
        arrays[f"in_{name}"] = a
        args[name] = nc.dram_tensor(f"in_{name}", a.shape, mybir.dt.from_np(a.dtype), kind="ExternalInput").ap()
    args["out"] = nc.dram_tensor("out_x", _OUT[0], F32, kind="ExternalOutput").ap()
    hybrid_trunk(nc, **args)
    r = run_bass_kernel_spmd(nc, [arrays], core_ids=[0])
    return r.results[0]["out_x"]
```
